# Optimizing a Trainium2 kernel written in Bass

```python
import math
import jax, jax.numpy as jnp
from jax import lax
import numpy as np

D_MODEL = 1024
BATCH = 1
SEQ = 512
DEPTH = 1

D_MIX = 2 * D_MODEL
SSD_INNER = D_MIX // 2
SSD_HEAD_DIM = 64
SSD_HEADS = SSD_INNER // SSD_HEAD_DIM
SSD_GROUPS = 2
SSD_HEADS_PER_GROUP = SSD_HEADS // SSD_GROUPS
SSD_STATE = 128
CONV_WIDTH = 4
CONV_DIM = SSD_INNER + 2 * SSD_GROUPS * SSD_STATE
CHUNK = 128
POOL_WINDOWS = (2, 4, 8, 16)
POOL_WIDTH = D_MIX - SSD_INNER
POOL_GROUP_DIM = POOL_WIDTH // len(POOL_WINDOWS)
IN_PROJ_DIM = SSD_INNER + CONV_DIM + SSD_HEADS + POOL_WIDTH
MEM_LEN = 256
XATTN_HEADS = 4
XATTN_HEAD_DIM = D_MODEL // XATTN_HEADS
D_FF = int(math.ceil((8 * D_MODEL / 3) / 256) * 256)
EPS = 1e-6


def rmsnorm(x, g):
    xf = x.astype(jnp.float32)
    y = xf * lax.rsqrt(jnp.mean(xf * xf, axis=-1, keepdims=True) + EPS)
    return (y * g.astype(jnp.float32)).astype(x.dtype)

def causal_depthwise_conv(u, w, b):
    k, c = w.shape
    out = lax.conv_general_dilated(
        u, w[:, None, :].astype(u.dtype), window_strides=(1,), padding=[(k - 1, 0)],
        dimension_numbers=("NWC", "WIO", "NWC"), feature_group_count=c)
    return out + b.astype(u.dtype)

def ssd_chunked(xs, dt, a, bm, cm):
    bsz, s, _, p = xs.shape
    nc = s // CHUNK
    g, hg, n = SSD_GROUPS, SSD_HEADS_PER_GROUP, SSD_STATE
    xc = (xs * dt[..., None]).reshape(bsz, nc, CHUNK, g, hg, p)
    adt = (dt * a).reshape(bsz, nc, CHUNK, g, hg).transpose(0, 3, 4, 1, 2)
    bc = bm.reshape(bsz, nc, CHUNK, g, n)
    cc = cm.reshape(bsz, nc, CHUNK, g, n)
    a_cs = jnp.cumsum(adt, axis=-1)
    causal = jnp.tril(jnp.ones((CHUNK, CHUNK), dtype=bool))
    seg = jnp.exp(jnp.where(causal, a_cs[..., :, None] - a_cs[..., None, :], -jnp.inf))
    cb = jnp.einsum("bclgn,bcsgn->bgcls", cc, bc)
    y_diag = jnp.einsum("bghcls,bcsghp->bclghp", cb[:, :, None] * seg, xc)
    decay_states = jnp.exp(a_cs[..., -1:] - a_cs)
    states = jnp.einsum("bcsgn,bghcs,bcsghp->bcghpn", bc, decay_states, xc)
    chunk_decay = jnp.exp(a_cs[..., -1])

    def step(carry, inp):
        st, dec = inp
        return dec[..., None, None] * carry + st, carry

    init = jnp.zeros((bsz, g, hg, p, n), jnp.float32)
    _, prev = lax.scan(step, init, (jnp.moveaxis(states, 1, 0), jnp.moveaxis(chunk_decay, -1, 0)))
    y_off = jnp.einsum("bclgn,cbghpn,bghcl->bclghp", cc, prev, jnp.exp(a_cs))
    return (y_diag + y_off).reshape(bsz, s, SSD_HEADS, p)

def multi_scale_pool(v, pool_w, pool_scale):
    bsz, s, _ = v.shape
    vg = v.astype(jnp.float32).reshape(bsz, s, len(POOL_WINDOWS), POOL_GROUP_DIM)
    cs0 = jnp.concatenate([jnp.zeros_like(vg[:, :1]), jnp.cumsum(vg, axis=1)], axis=1)
    pos1 = jnp.arange(1, s + 1, dtype=jnp.float32)
    outs = []
    for gi, w in enumerate(POOL_WINDOWS):
        c = cs0[:, :, gi]
        lower = jnp.pad(c[:, :s + 1 - w], ((0, 0), (w - 1, 0), (0, 0)))
        count = jnp.minimum(pos1, float(w))[None, :, None]
        outs.append((c[:, 1:] - lower) / count - vg[:, :, gi])
    d = jnp.stack(outs, axis=2)
    out = jnp.einsum("bsgc,gcd->bsgd", d, pool_w.astype(jnp.float32)).reshape(bsz, s, POOL_WIDTH)
    return (out * pool_scale.astype(jnp.float32)).astype(v.dtype)

def hybrid_mixer(u, w_in, conv_w, conv_b, dt_bias, a_log, d_skip, ssd_norm, pool_w, pool_scale, w_out):
    bsz, s, _ = u.shape
    proj = u @ w_in
    z, xbc, dt_raw, v = jnp.split(
        proj, [SSD_INNER, SSD_INNER + CONV_DIM, SSD_INNER + CONV_DIM + SSD_HEADS], axis=-1)
    xbc = jax.nn.silu(causal_depthwise_conv(xbc, conv_w, conv_b)).astype(jnp.float32)
    xs, bm, cm = jnp.split(xbc, [SSD_INNER, SSD_INNER + SSD_GROUPS * SSD_STATE], axis=-1)
    xs = xs.reshape(bsz, s, SSD_HEADS, SSD_HEAD_DIM)
    bm = bm.reshape(bsz, s, SSD_GROUPS, SSD_STATE)
    cm = cm.reshape(bsz, s, SSD_GROUPS, SSD_STATE)
    dt = jax.nn.softplus(dt_raw.astype(jnp.float32) + dt_bias.astype(jnp.float32))
    a = -jnp.exp(a_log.astype(jnp.float32))
    y = ssd_chunked(xs, dt, a, bm, cm)
    y = y + d_skip.astype(jnp.float32)[:, None] * xs
    y = y.reshape(bsz, s, SSD_INNER) * jax.nn.silu(z.astype(jnp.float32))
    y_ssd = rmsnorm(y, ssd_norm).astype(u.dtype)
    y_pool = multi_scale_pool(v, pool_w, pool_scale)
    return jnp.concatenate([y_ssd, y_pool], axis=-1) @ w_out

def memory_cross_attention(q_in, m_in, w_q, w_kv, w_o):
    bsz, s, _ = q_in.shape
    q = (q_in @ w_q).reshape(bsz, s, XATTN_HEADS, XATTN_HEAD_DIM)
    k, v = jnp.split(m_in @ w_kv, 2, axis=-1)
    k = k.reshape(bsz, -1, XATTN_HEADS, XATTN_HEAD_DIM)
    v = v.reshape(bsz, -1, XATTN_HEADS, XATTN_HEAD_DIM)
    scores = jnp.einsum("bshd,bmhd->bhsm", q.astype(jnp.float32), k.astype(jnp.float32))
    probs = jax.nn.softmax(scores * (XATTN_HEAD_DIM ** -0.5), axis=-1).astype(v.dtype)
    o = jnp.einsum("bhsm,bmhd->bshd", probs, v).reshape(bsz, s, D_MODEL)
    return o @ w_o

def swiglu(u, w_gate_up, w_down):
    gate, up = jnp.split(u @ w_gate_up, 2, axis=-1)
    return (jax.nn.silu(gate) * up) @ w_down

def first_inputs(seed: int = 0) -> dict:
    key = jax.random.key(seed)
    ks = iter(jax.random.split(key, 32))
    f32 = jnp.float32

    def nrm(shape, fan_in):
        return jax.random.normal(next(ks), shape, f32) * (fan_in ** -0.5)

    def gain(shape):
        return 1.0 + 0.02 * jax.random.normal(next(ks), shape, f32)

    L = DEPTH
    x = jax.random.normal(next(ks), (BATCH, SEQ, D_MODEL), f32)
    mem = jax.random.normal(next(ks), (BATCH, MEM_LEN, D_MODEL), f32)
    dt0 = jnp.exp(jax.random.uniform(next(ks), (L, SSD_HEADS), f32, math.log(1e-3), math.log(1e-1)))
    dt_bias = dt0 + jnp.log(-jnp.expm1(-dt0))
    a_log = jnp.log(jax.random.uniform(next(ks), (L, SSD_HEADS), f32, 1.0, 16.0))
    return {
        "x": x,
        "mem": mem,
        "mix_norm": gain((L, D_MODEL)),
        "w_in": nrm((L, D_MODEL, IN_PROJ_DIM), D_MODEL),
        "conv_w": nrm((L, CONV_WIDTH, CONV_DIM), CONV_WIDTH),
        "conv_b": 0.02 * jax.random.normal(next(ks), (L, CONV_DIM), f32),
        "dt_bias": dt_bias,
        "a_log": a_log,
        "d_skip": gain((L, SSD_HEADS)),
        "ssd_norm": gain((L, SSD_INNER)),
        "pool_w": nrm((L, len(POOL_WINDOWS), POOL_GROUP_DIM, POOL_GROUP_DIM), POOL_GROUP_DIM),
        "pool_scale": gain((L, POOL_WIDTH)),
        "w_out_mix": nrm((L, D_MIX, D_MODEL), D_MIX),
        "xattn_norm": gain((L, D_MODEL)),
        "mem_norm": gain((L, D_MODEL)),
        "w_q": nrm((L, D_MODEL, D_MODEL), D_MODEL),
        "w_kv": nrm((L, D_MODEL, 2 * D_MODEL), D_MODEL),
        "w_o": nrm((L, D_MODEL, D_MODEL), D_MODEL),
        "ffn_norm": gain((L, D_MODEL)),
        "w_gate_up": nrm((L, D_MODEL, 2 * D_FF), D_MODEL),
        "w_down": nrm((L, D_FF, D_MODEL), D_FF),
        "final_norm": gain((D_MODEL,)),
    }

def first_block(x, mem, mix_norm, w_in, conv_w, conv_b, dt_bias, a_log, d_skip, ssd_norm,
              pool_w, pool_scale, w_out_mix, xattn_norm, mem_norm, w_q, w_kv, w_o,
              ffn_norm, w_gate_up, w_down, final_norm):
    h = x
    for l in range(DEPTH):
        h = h + hybrid_mixer(rmsnorm(h, mix_norm[l]), w_in[l], conv_w[l], conv_b[l], dt_bias[l],
                             a_log[l], d_skip[l], ssd_norm[l], pool_w[l], pool_scale[l], w_out_mix[l])
        h = h + memory_cross_attention(rmsnorm(h, xattn_norm[l]), rmsnorm(mem, mem_norm[l]),
                                       w_q[l], w_kv[l], w_o[l])
        h = h + swiglu(rmsnorm(h, ffn_norm[l]), w_gate_up[l], w_down[l])
    return rmsnorm(h, final_norm)


DEPTH_2 = 2

N_A_LAYERS = DEPTH_2 // 2
N_B_LAYERS = DEPTH_2 - N_A_LAYERS
HEAD_DIM = 64
SB_HEADS = D_MODEL // HEAD_DIM
NSA_HEADS = D_MODEL // HEAD_DIM
NSA_KV_GROUPS = 4
NSA_HPG = NSA_HEADS // NSA_KV_GROUPS
CMP_LEN = 32
CMP_STRIDE = 16
CMP_HIDDEN = 256
SEL_LEN = 64
SEL_TOPK = 16
WINDOW = 512
D_FF_2 = 4 * D_MODEL
ROPE_THETA = 500000.0
ROT_DIM = HEAD_DIM // 4
Q_BLOCK = 128
NORM_EPS = 1e-5
NEG = -1e30
FORCED_SCORE = 1e6


def rms_norm(x, g):
    xf = x.astype(jnp.float32)
    y = xf * lax.rsqrt(jnp.mean(xf * xf, axis=-1, keepdims=True) + NORM_EPS)
    return (y * g.astype(jnp.float32)).astype(x.dtype)

def partial_rope(x):
    s = x.shape[1]
    half = ROT_DIM // 2
    inv_freq = ROPE_THETA ** (-jnp.arange(half, dtype=jnp.float32) * 2.0 / ROT_DIM)
    ang = jnp.arange(s, dtype=jnp.float32)[:, None] * inv_freq[None, :]
    cos = jnp.cos(ang)[None, :, None, :]
    sin = jnp.sin(ang)[None, :, None, :]
    xr = x[..., :ROT_DIM].astype(jnp.float32)
    x1, x2 = xr[..., :half], xr[..., half:]
    rot = jnp.concatenate([x1 * cos - x2 * sin, x2 * cos + x1 * sin], axis=-1).astype(x.dtype)
    return jnp.concatenate([rot, x[..., ROT_DIM:]], axis=-1)

def to_qblocks(a):
    b, s = a.shape[0], a.shape[1]
    return jnp.moveaxis(a.reshape((b, s // Q_BLOCK, Q_BLOCK) + a.shape[2:]), 1, 0)

def from_qblocks(a):
    a = jnp.moveaxis(a, 0, 1)
    return a.reshape((a.shape[0], a.shape[1] * a.shape[2]) + a.shape[3:])

def sqrelu_mlp(x, w1, w2):
    h = jax.nn.relu(x @ w1)
    return (h * h) @ w2

def stick_breaking_attention(h, w_qkv, w_o):
    b, s, _ = h.shape
    n_qb = s // Q_BLOCK
    qkv = (h @ w_qkv).reshape(b, s, 3, SB_HEADS, HEAD_DIM)
    q, k, v = qkv[:, :, 0], qkv[:, :, 1], qkv[:, :, 2]
    scale = HEAD_DIM ** -0.5
    key_pos = jnp.arange(s)

    def block(args):
        qi, q_blk = args
        t = qi * Q_BLOCK + jnp.arange(Q_BLOCK)
        z = jnp.einsum('bqhd,bshd->bhqs', q_blk, k).astype(jnp.float32) * scale
        causal = key_pos[None, :] < t[:, None]
        log_1m = jnp.where(causal, jax.nn.log_sigmoid(-z), 0.0)
        excl = lax.cumsum(log_1m, axis=3, reverse=True) - log_1m
        a = jnp.where(causal, jnp.exp(jax.nn.log_sigmoid(z) + excl), 0.0)
        return jnp.einsum('bhqs,bshd->bqhd', a.astype(v.dtype), v)

    o = lax.map(block, (jnp.arange(n_qb), to_qblocks(q)))
    return from_qblocks(o).reshape(b, s, SB_HEADS * HEAD_DIM) @ w_o

def nsa_shared_kv(h, kv_norm, w_kv, cmp_pos, cmp_w1, cmp_w2):
    b, s, _ = h.shape
    hn = rms_norm(h, kv_norm)
    kv = (hn @ w_kv).reshape(b, s, 3, 2, NSA_KV_GROUPS, HEAD_DIM)
    n_cmp = (s - CMP_LEN) // CMP_STRIDE + 1
    idx = jnp.arange(n_cmp)[:, None] * CMP_STRIDE + jnp.arange(CMP_LEN)[None, :]
    blk = kv[:, :, 0][:, idx]
    blk = blk + jnp.transpose(cmp_pos, (1, 0, 2))[None, None, :, :, None, :]
    blk = jnp.transpose(blk, (0, 1, 3, 4, 2, 5)).reshape(b, n_cmp, 2, NSA_KV_GROUPS, CMP_LEN * HEAD_DIM)
    hid = jax.nn.gelu(jnp.einsum('bncgf,cfe->bncge', blk, cmp_w1))
    cmp = jnp.einsum('bncge,ced->bncgd', hid, cmp_w2)
    k_cmp, v_cmp = cmp[:, :, 0], cmp[:, :, 1]
    k_slc, v_slc = partial_rope(kv[:, :, 1, 0]), kv[:, :, 1, 1]
    k_win, v_win = partial_rope(kv[:, :, 2, 0]), kv[:, :, 2, 1]
    return (k_cmp, v_cmp, k_slc, v_slc, k_win, v_win)

def nsa_attention(h, w_q, gate_b, w_o, shared):
    k_cmp, v_cmp, k_slc, v_slc, k_win, v_win = shared
    b, s, _ = h.shape
    G, HPG, DH = NSA_KV_GROUPS, NSA_HPG, HEAD_DIM
    n_cmp = k_cmp.shape[1]
    n_sel = s // SEL_LEN
    n_qb = s // Q_BLOCK
    topk = min(SEL_TOPK, n_sel)
    scale = DH ** -0.5

    proj = h @ w_q
    q = proj[..., :NSA_HEADS * DH].reshape(b, s, NSA_HEADS, DH)
    gates = jax.nn.sigmoid((proj[..., NSA_HEADS * DH:] + gate_b).astype(jnp.float32)).reshape(b, s, 3, NSA_HEADS)
    q_rot = partial_rope(q)

    cmp_start = jnp.arange(n_cmp) * CMP_STRIDE
    cmp_end = cmp_start + CMP_LEN - 1
    sel_ids = jnp.arange(n_sel)
    sel_start = sel_ids * SEL_LEN
    overlap = ((cmp_start[:, None] < sel_start[None, :] + SEL_LEN)
               & (cmp_start[:, None] + CMP_LEN > sel_start[None, :])).astype(jnp.float32)
    k_sel_blocks = jnp.transpose(k_slc.reshape(b, n_sel, SEL_LEN, G, DH), (0, 3, 1, 2, 4))
    v_sel_blocks = jnp.transpose(v_slc.reshape(b, n_sel, SEL_LEN, G, DH), (0, 3, 1, 2, 4))
    pad = ((0, 0), (WINDOW, 0), (0, 0), (0, 0))
    k_win_p = jnp.pad(k_win, pad)
    v_win_p = jnp.pad(v_win, pad)
    gather = jax.vmap(jax.vmap(lambda blocks, ids: blocks[ids]))

    def block(args):
        qi, q_blk, qr_blk = args
        q0 = qi * Q_BLOCK
        t = q0 + jnp.arange(Q_BLOCK)
        qg = q_blk.reshape(b, Q_BLOCK, G, HPG, DH)
        qrg = qr_blk.reshape(b, Q_BLOCK, G, HPG, DH)

        sc = jnp.einsum('bqghd,bngd->bghqn', qg, k_cmp).astype(jnp.float32) * scale
        valid_c = cmp_end[None, :] <= t[:, None]
        p_cmp = jax.nn.softmax(jnp.where(valid_c, sc, NEG), axis=-1)
        p_cmp = p_cmp * jnp.any(valid_c, axis=-1)[:, None]
        o_cmp = jnp.einsum('bghqn,bngd->bqghd', p_cmp.astype(v_cmp.dtype), v_cmp)

        imp = jnp.einsum('bghqn,nm->bgqm', p_cmp, overlap)
        blk_t = t // SEL_LEN
        forced = (sel_ids[None, :] == 0) | (sel_ids[None, :] == blk_t[:, None]) | (sel_ids[None, :] == blk_t[:, None] - 1)
        causal_b = sel_ids[None, :] <= blk_t[:, None]
        imp = jnp.where(causal_b, jnp.where(forced, FORCED_SCORE, imp), -jnp.inf)
        _, top_idx = lax.top_k(imp, topk)
        k_sel = gather(k_sel_blocks, top_idx)
        v_sel = gather(v_sel_blocks, top_idx)
        ss = jnp.einsum('bqghd,bgqkld->bghqkl', qrg, k_sel).astype(jnp.float32) * scale
        key_pos = top_idx[..., None] * SEL_LEN + jnp.arange(SEL_LEN)
        valid_s = key_pos <= t[None, None, :, None, None]
        ss = jnp.where(valid_s[:, :, None], ss, NEG)
        p_sel = jax.nn.softmax(ss.reshape(b, G, HPG, Q_BLOCK, topk * SEL_LEN), axis=-1).reshape(ss.shape)
        o_sel = jnp.einsum('bghqkl,bgqkld->bqghd', p_sel.astype(v_sel.dtype), v_sel)

        k_w = lax.dynamic_slice_in_dim(k_win_p, q0, WINDOW + Q_BLOCK, axis=1)
        v_w = lax.dynamic_slice_in_dim(v_win_p, q0, WINDOW + Q_BLOCK, axis=1)
        sw = jnp.einsum('bqghd,bsgd->bghqs', qrg, k_w).astype(jnp.float32) * scale
        kpos = q0 - WINDOW + jnp.arange(WINDOW + Q_BLOCK)
        diff = t[:, None] - kpos[None, :]
        valid_w = (diff >= 0) & (diff < WINDOW) & (kpos[None, :] >= 0)
        p_w = jax.nn.softmax(jnp.where(valid_w, sw, NEG), axis=-1)
        o_win = jnp.einsum('bghqs,bsgd->bqghd', p_w.astype(v_w.dtype), v_w)

        return jnp.stack([o_cmp, o_sel, o_win], axis=2).reshape(b, Q_BLOCK, 3, NSA_HEADS, DH)

    o = from_qblocks(lax.map(block, (jnp.arange(n_qb), to_qblocks(q), to_qblocks(q_rot))))
    out = jnp.einsum('bsch,bschd->bshd', gates.astype(o.dtype), o).reshape(b, s, NSA_HEADS * DH)
    return out @ w_o

def second_inputs(seed: int = 0) -> dict:
    key = jax.random.key(seed)
    ks = jax.random.split(key, 16)
    f32 = jnp.float32

    def w(k, shape, fan_in):
        return jax.random.normal(k, shape, f32) * fan_in ** -0.5

    x = jax.random.normal(ks[0], (BATCH, SEQ, D_MODEL), f32)
    norm_gain = 1.0 + 0.02 * jax.random.normal(ks[1], (DEPTH_2, 2, D_MODEL), f32)
    sb_w_qkv = w(ks[2], (N_A_LAYERS, D_MODEL, 3 * SB_HEADS * HEAD_DIM), D_MODEL)
    sb_w_o = w(ks[3], (N_A_LAYERS, SB_HEADS * HEAD_DIM, D_MODEL), SB_HEADS * HEAD_DIM)
    kv_norm = 1.0 + 0.02 * jax.random.normal(ks[4], (D_MODEL,), f32)
    nsa_w_kv = w(ks[5], (D_MODEL, 3 * 2 * NSA_KV_GROUPS * HEAD_DIM), D_MODEL)
    cmp_pos = 0.1 * jax.random.normal(ks[6], (2, CMP_LEN, HEAD_DIM), f32)
    cmp_w1 = w(ks[7], (2, CMP_LEN * HEAD_DIM, CMP_HIDDEN), CMP_LEN * HEAD_DIM)
    cmp_w2 = w(ks[8], (2, CMP_HIDDEN, HEAD_DIM), CMP_HIDDEN)
    nsa_w_q = w(ks[9], (N_B_LAYERS, D_MODEL, NSA_HEADS * HEAD_DIM + 3 * NSA_HEADS), D_MODEL)
    nsa_gate_b = 0.1 * jax.random.normal(ks[10], (N_B_LAYERS, 3 * NSA_HEADS), f32)
    nsa_w_o = w(ks[11], (N_B_LAYERS, NSA_HEADS * HEAD_DIM, D_MODEL), NSA_HEADS * HEAD_DIM)
    mlp_w1 = w(ks[12], (DEPTH_2, D_MODEL, D_FF_2), D_MODEL)
    mlp_w2 = w(ks[13], (DEPTH_2, D_FF_2, D_MODEL), D_FF_2)
    final_norm = 1.0 + 0.02 * jax.random.normal(ks[14], (D_MODEL,), f32)
    return {"x": x, "norm_gain": norm_gain, "sb_w_qkv": sb_w_qkv, "sb_w_o": sb_w_o,
            "kv_norm": kv_norm, "nsa_w_kv": nsa_w_kv, "cmp_pos": cmp_pos, "cmp_w1": cmp_w1,
            "cmp_w2": cmp_w2, "nsa_w_q": nsa_w_q, "nsa_gate_b": nsa_gate_b, "nsa_w_o": nsa_w_o,
            "mlp_w1": mlp_w1, "mlp_w2": mlp_w2, "final_norm": final_norm}

def second_block(x, norm_gain, sb_w_qkv, sb_w_o, kv_norm, nsa_w_kv, cmp_pos, cmp_w1, cmp_w2,
              nsa_w_q, nsa_gate_b, nsa_w_o, mlp_w1, mlp_w2, final_norm):
    h = x
    shared = None
    for layer in range(DEPTH_2):
        hn = rms_norm(h, norm_gain[layer, 0])
        if layer < N_A_LAYERS:
            h = h + stick_breaking_attention(hn, sb_w_qkv[layer], sb_w_o[layer])
        else:
            j = layer - N_A_LAYERS
            h = h + nsa_attention(hn, nsa_w_q[j], nsa_gate_b[j], nsa_w_o[j], shared)
        h = h + sqrelu_mlp(rms_norm(h, norm_gain[layer, 1]), mlp_w1[layer], mlp_w2[layer])
        if layer == N_A_LAYERS - 1:
            shared = nsa_shared_kv(h, kv_norm, nsa_w_kv, cmp_pos, cmp_w1, cmp_w2)
    return rms_norm(h, final_norm)


def setup_inputs(seed=0):
    out = dict(first_inputs(seed))
    for name, value in second_inputs(seed + 1).items():
        if name != "x":
            out[name + "_2"] = value
    return out


def reference(
    x, mem, mix_norm, w_in, conv_w, conv_b, dt_bias, a_log, d_skip, ssd_norm, pool_w,
    pool_scale, w_out_mix, xattn_norm, mem_norm, w_q, w_kv, w_o, ffn_norm, w_gate_up, w_down,
    final_norm, norm_gain_2, sb_w_qkv_2, sb_w_o_2, kv_norm_2, nsa_w_kv_2, cmp_pos_2, cmp_w1_2,
    cmp_w2_2, nsa_w_q_2, nsa_gate_b_2, nsa_w_o_2, mlp_w1_2, mlp_w2_2, final_norm_2,
):
    x = first_block(
        x, mem, mix_norm, w_in, conv_w, conv_b, dt_bias, a_log, d_skip, ssd_norm, pool_w,
        pool_scale, w_out_mix, xattn_norm, mem_norm, w_q, w_kv, w_o, ffn_norm, w_gate_up,
        w_down, final_norm,
    )
    return second_block(
        x, norm_gain_2, sb_w_qkv_2, sb_w_o_2, kv_norm_2, nsa_w_kv_2, cmp_pos_2, cmp_w1_2,
        cmp_w2_2, nsa_w_q_2, nsa_gate_b_2, nsa_w_o_2, mlp_w1_2, mlp_w2_2, final_norm_2,
    )


_drawn_inputs = setup_inputs


def setup_inputs(seed=0):
    import zlib

    import numpy as np

    out = dict(_drawn_inputs(seed))
    spreads = {}
    factors = {'conv_b': 2.851,
     'd_skip': 6.62,
     'ssd_norm': 4.462,
     'pool_scale': 4.826,
     'xattn_norm': 8.0,
     'mem_norm': 8.0,
     'ffn_norm': 4.197,
     'kv_norm_2': 8.0,
     'cmp_pos_2': 2.78,
     'nsa_gate_b_2': 7.194,
     'final_norm_2': 2.87}
    for name, (base, spread) in spreads.items():
        noise = np.random.default_rng([zlib.crc32(name.encode()), seed]).standard_normal(out[name].shape)
        drawn = base * np.exp(spread * noise) if base else spread * noise
        out[name] = __import__('jax').numpy.asarray(drawn.astype(out[name].dtype))
    for name, factor in factors.items():
        out[name] = (out[name] * factor).astype(out[name].dtype)
    return out
```

```python
import concourse.bass as bass
from concourse import mybir
import numpy as np

F = mybir.dt.float32
R = mybir.dt.float32r
BF = mybir.dt.bfloat16
ALU = mybir.AluOpType
ACT = mybir.ActivationFunctionType
AX = mybir.AxisListType

S, D, ML = 512, 1024, 256
NEG = -1.0e30

COLS = {}
_at = 0
for _n, _w in [("mix_norm", 8), ("conv_w", 48), ("conv_b", 12), ("ssd_norm", 8), ("pool_scale", 8),
               ("xattn_norm", 8), ("mem_norm", 8), ("ffn_norm", 8), ("kv_norm", 8), ("ng", 32),
               ("first", 8), ("final", 8), ("d_skip", 8), ("cmp_pos", 32), ("dt_bias", 16), ("a_log", 16),
               ("gate_b", 48)]:
    COLS[_n] = (_at, _w)
    _at += _w
NCOLS = _at

CONST = {}
_at = 0
for _n, _w in [("I", 128), ("TU", 128), ("TRI", 128), ("NONES", 128), ("ONES", 128), ("NEGT", 128),
               ("NEGC", 128), ("NEGS", 128), ("MS", 128), ("LAST", 128), ("CNT", 64), ("NEGM", 128),
               ("P", 128), ("D0", 128), ("D1", 128), ("PD0", 128), ("PD1", 128), ("RC", 512), ("RS", 512)]:
    CONST[_n] = (_at, _w)
    _at += _w
NCONST = _at


def constants():
    c = np.zeros((128, NCONST), np.float32)

    def put(name, a):
        at, w = CONST[name]
        c[:, at:at + w] = a

    i = np.arange(128)
    put("I", np.eye(128))
    put("TU", i[:, None] <= i[None, :])
    put("TRI", -1.0 * (i[:, None] >= i[None, :]))
    put("NONES", -1.0)
    put("ONES", 1.0)
    put("NEGT", NEG * (i[:, None] > i[None, :]))
    put("NEGC", NEG * (i[None, :] > i[:, None]))
    put("NEGS", NEG * (i[:, None] >= i[None, :]))
    put("MS", i[:, None] < i[None, :])
    put("LAST", (i[:, None] == 127) * np.ones((1, 128)))
    P = np.zeros((128, 128), np.float32)
    for base in (0, 64):
        for j in range(8):
            P[base + j + 8, base + j] = -1.0
            P[base + j, base + j + 8] = 1.0
    put("P", P)
    for g in range(2):
        Dg = np.zeros((128, 128), np.float32)
        for j in range(128):
            Dg[64 * g + j % 64, j] = 1.0
        put(f"D{g}", Dg)
        put(f"PD{g}", P @ Dg)
    for n, w in enumerate((2, 4, 8, 16)):
        at = CONST["CNT"][0] + 16 * n
        c[:, at:at + w] = np.float32(w) / np.arange(1, w + 1, dtype=np.float32)
    n = np.arange(32)
    for b in range(4):
        t = 128 * b + i
        at = CONST["NEGM"][0] + 32 * b
        c[:, at:at + 32] = NEG * ((16 * n + 31)[None, :] > t[:, None])
    inv = np.float32(500000.0) ** (-np.arange(8, dtype=np.float32) * np.float32(2.0) / np.float32(16))
    ang = np.arange(S, dtype=np.float32)[None, :] * inv[:, None].astype(np.float32)
    rc = np.ones((128, S), np.float32)
    rs = np.zeros((128, S), np.float32)
    for base in (0, 64):
        for o in (0, 8):
            rc[base + o:base + o + 8] = np.cos(ang)
            rs[base + o:base + o + 8] = np.sin(ang)
    put("RC", rc)
    put("RS", rs)
    return c


class Queue:

    def __init__(self, sem):
        self.sem, self.n, self.ops, self.seen = sem, 0, [], {}

    def wait(self, *tokens):
        for t in tokens:
            if t is None:
                continue
            if isinstance(t, list):
                self.wait(*t)
                continue
            sem, v = t
            if self.seen.get(sem.name, 0) < v:
                self.seen[sem.name] = v
                self.ops.append(lambda e, sem=sem, v=v: e.wait_ge(sem, v))

    def do(self, f):
        self.n += 1
        self.ops.append(lambda e: f(e).then_inc(self.sem, 1))
        return (self.sem, self.n)

    def plain(self, f):
        self.ops.append(f)

    def dma(self, sem, f):
        sem[1] += 16
        self.ops.append(lambda e, s=sem[0]: f(e).then_inc(s, 16))
        return (sem[0], sem[1])

    def now(self):
        return (self.sem, self.n) if self.n else None


class Buf:

    def __init__(self, t):
        self.t, self.last, self.live = t, [], False

    @property
    def free(self):
        return self.last

    @free.setter
    def free(self, tokens):
        self.last, self.live = tokens, False

    def take(self, *qs):
        assert not self.live
        for q in qs:
            q.wait(*self.last)
        self.last, self.live = [], True
        return self.t


class Ring:
    def __init__(self, bufs):
        self.bufs, self.i = bufs, 0

    def next(self):
        b = self.bufs[self.i % len(self.bufs)]
        self.i += 1
        return b


class Pair:

    def __init__(self, hi, lo, n):
        self.hi, self.lo, self.tok, self.free = hi, lo, [None] * n, [[] for _ in range(n)]


def program(nc, A, cols_d, const_d, out_d, stop=None):
    NR, NH = 5, 3
    base = [(nc.sbuf_base + 63) // 64 * 64]
    limit = nc.sbuf_usable_end

    def place(at, name, shape, dt=F):
        return nc.alloc_sbuf_tensor_at(name, shape, dt, offset=at)

    def size(shape, dt=F):
        n = 4 if dt != BF else 2
        for x in shape[1:]:
            n *= x
        return (n + 63) // 64 * 64

    def sb(name, shape, dt=F):
        t = place(base[0], name, shape, dt)
        base[0] += size(shape, dt)
        assert base[0] <= limit, (name, base[0], limit)
        return t

    class Phase:

        def __init__(self, at, tag):
            self.at, self.tag = at, tag

        def sb(self, name, shape, dt=F):
            t = place(self.at, f"{self.tag}_{name}", shape, dt)
            self.at += size(shape, dt)
            assert self.at <= limit, (name, self.at, limit)
            return t

    sems = {}

    def sem(name):
        sems[name] = nc.alloc_semaphore(name)
        return sems[name]

    PE, V, AC, PL, SP = (Queue(sem(f"done_{n}")) for n in ("pe", "dve", "act", "pool", "sp"))

    cols = sb("cols", [128, NCOLS])
    cst = sb("cst", [128, CONST["P"][0]])
    maskb = sb("maskb", [128, 4, 128], BF)
    Ib = sb("Ib", [128, 128], BF)
    small = sb("small", [128, 64])
    trir = sb("trir", [128, 2, 128], R)
    H = sb("H", [128, 8, S])
    RAW = [sb(f"raw{i}", [128, 1024]) for i in range(NR)]
    WH = [sb(f"wh{i}", [128, 1024], R) for i in range(NH)]
    WL = [sb(f"wl{i}", [128, 1024], R) for i in range(NH)]
    XH = sb("XH", [128, 8, S], R)
    XL = sb("XL", [128, 8, S], R)
    rs = Buf(sb("rs", [128, S]))
    sqr = Ring([Buf(sb(f"sq{i}", [128, S])) for i in range(2)])
    tmp = Ring([Buf(sb(f"tmp{i}", [128, S])) for i in range(4)])
    nrms = sb("nrms", [128, 80])
    sb_small = sb("sb_small", [128, 64])
    PH0 = base[0]
    X = Pair(XH, XL, 8)
    PS = [Buf(nc.alloc_psum_tensor(f"ps{i}", [128, 512], F)) for i in range(8)]
    psr = Ring(PS[0:7])
    NB = PS[7]

    def col(name, k, n=1, p=128):
        at, _ = COLS[name]
        return cols[0:p, at + k:at + k + n]

    def con(name, p0=0, p1=128, a=0, b=None):
        at, w = CONST[name]
        return cst[p0:p1, at + a:at + (w if b is None else b)]

    def dsem(name):
        return [sem(name), 0]

    U = []

    def unit(name, ap):
        U.append((name, ap))

    def wcols(w, c0, n=128, r0=0, r1=None):
        v = w[r0:(r1 if r1 is not None else w.shape[0]), :].rearrange("(k p) n -> p k n", p=128)
        return v[:, :, c0:c0 + n]

    w_in, w_out = A["w_in"][0], A["w_out_mix"][0]
    for k in range(8):
        unit(f"v{k}", wcols(w_in, 2576 + 128 * k))
    unit("dt", wcols(w_in, 2560))
    def unit_pool(half):
        for g in (2 * half, 2 * half + 1):
            unit(f"pool{g}", wcols(A["pool_w"][0, g], 0, 256))

    def unit_out_pool(half):
        for o in range(4):
            unit(f"op{half}{o}", wcols(w_out, 256 * o, 256, 1024 + 512 * half, 1536 + 512 * half))

    unit_pool(0)
    for k in range(8, 12):
        unit(f"xbc{k}", wcols(w_in, 1024 + 128 * k))
    unit_out_pool(0)
    unit_pool(1)
    for k in range(8):
        unit(f"xbc{k}", wcols(w_in, 1024 + 128 * k))
        if k == 1:
            unit_out_pool(1)
    for k in range(8):
        unit(f"z{k}", wcols(w_in, 128 * k))
    for o in range(8):
        unit(f"os{o}", wcols(w_out, 128 * o, 128, 0, 1024))
    w_kv = A["w_kv"][0]
    for o in range(8):
        unit(f"mk{o}", wcols(w_kv, 128 * o))
    for b in range(2):
        for kk in range(4):
            unit(f"mv{b}{kk}", wcols(w_kv, 1024 + 512 * b, 512, 256 * kk, 256 * kk + 256))
    for o in range(8):
        unit(f"xq{o}", wcols(A["w_q"][0], 128 * o))
    for o in range(8):
        unit(f"xo{o}", wcols(A["w_o"][0], 128 * o))
    GU = [4, 4, 4, 4, 4, 2]
    wgu, wdn = A["w_gate_up"][0], A["w_down"][0]

    def ffn_order(groups):
        out = []
        for g in range(len(groups) + 1):
            if g < len(groups):
                out.append(("up", g))
            if g >= 1:
                out.append(("down", g - 1))
        return out

    def down_units(tag, w, g, c0, n):
        if n == 4:
            for o in range(4):
                unit(f"{tag}d{g}_{o}", wcols(w, 256 * o, 256, 128 * c0, 128 * (c0 + 4)))
        else:
            for o in range(2):
                unit(f"{tag}d{g}_{o}", wcols(w, 512 * o, 512, 128 * c0, 128 * (c0 + 2)))

    for kind, g in ffn_order(GU):
        c0 = sum(GU[:g])
        if kind == "up":
            for c in range(c0, c0 + GU[g]):
                unit(f"fg{c}", wcols(wgu, 128 * c))
                unit(f"fu{c}", wcols(wgu, 2816 + 128 * c))
        else:
            down_units("f", wdn, g, c0, GU[g])
    sbq = A["sb_w_qkv_2"][0]
    for o in range(16):
        unit(f"sq{o}", wcols(sbq, 128 * o))
    for b in range(2):
        for kk in range(4):
            unit(f"sv{b}{kk}", wcols(sbq, 2048 + 512 * b, 512, 256 * kk, 256 * kk + 256))
    for o in range(8):
        unit(f"so{o}", wcols(A["sb_w_o_2"][0], 128 * o))

    def mlp_units(tag, l):
        for kind, g in ffn_order([4] * 8):
            if kind == "up":
                for c in range(4 * g, 4 * g + 4):
                    unit(f"{tag}u{c}", wcols(A["mlp_w1_2"][l], 128 * c))
            else:
                down_units(tag, A["mlp_w2_2"][l], g, 4 * g, 4)

    mlp_units("m", 0)
    nq = A["nsa_w_q_2"][0]
    for o in range(8):
        unit(f"nq{o}", wcols(nq, 128 * o))
    unit("ng", wcols(nq, 1024, 48))
    nkv = A["nsa_w_kv_2"]
    for o in range(4):
        unit(f"nc{o}", wcols(nkv, 128 * o))
    for kind in range(2):
        for o in range(2):
            unit(f"nk{kind}{o}", wcols(nkv, 512 + 512 * kind + 128 * o))
    for kind in range(2):
        for kk in range(2):
            unit(f"nv{kind}{kk}", wcols(nkv, 768 + 512 * kind, 256, 512 * kk, 512 * kk + 512))
    for c in range(2):
        for j in range(4):
            unit(f"c1{c}{j}", wcols(A["cmp_w1_2"][c], 0, 256, 512 * j, 512 * j + 512))
    for o in range(8):
        unit(f"no{o}", wcols(A["nsa_w_o_2"][0], 128 * o))
    mlp_units("n", 1)

    wsem = [dsem(f"w_in_{i}") for i in range(NR)]
    loaded, hi_done, lo_done, used = {}, {}, {}, {}
    at = [0, 0]

    def shaped(t, ap):
        n = ap.shape[1] * ap.shape[2]
        return t[:, 0:n].rearrange("p (k n) -> p k n", k=ap.shape[1])

    def issue(i):
        if i >= len(U):
            return
        if i >= NR:
            SP.wait(hi_done[i - NR], lo_done[i - NR])
        ap = U[i][1]
        loaded[i] = SP.dma(wsem[i % NR], lambda e: e.dma_start(shaped(RAW[i % NR], ap), ap))

    def prepare(i):
        if i >= len(U):
            return
        raw, wh, wl = (shaped(t, U[i][1]) for t in (RAW[i % NR], WH[i % NH], WL[i % NH]))
        for q in (AC, V):
            q.wait(loaded[i])
            if i >= NH:
                q.wait(used[i - NH])
        hi_done[i] = AC.do(lambda e: e.copy(wh, raw))
        V.wait(hi_done[i])
        lo_done[i] = V.do(lambda e: e.tensor_tensor(wl, raw, wh.bitcast(F), ALU.subtract))
        issue(i + NR)

    def weights(name):
        i = at[0]
        at[0] += 1
        assert U[i][0] == name, (U[i][0], name)
        while at[1] < min(i + 3, len(U)):
            prepare(at[1])
            at[1] += 1
        PE.wait(lo_done[i])
        return i, shaped(WH[i % NH], U[i][1]), shaped(WL[i % NH], U[i][1])

    def spent(i, tok):
        used[i] = tok

    def mm(out, a, b, start, stop):
        return lambda e: e.matmul(out, a, b, start=start, stop=stop, skip_group_check=True)

    def mm3(out, a, b, start=False, stop=False):
        PE.plain(mm(out, a[0], b[0], start, False))
        PE.plain(mm(out, a[0], b[1], False, False))
        return mm(out, a[1], b[0], False, stop)

    def project(name, x, bank, nk=8, c=0, k0=0, n=S):
        i, wh, wl = weights(name) if isinstance(name, str) else name
        out = bank.take(PE)[:, 0:n]
        for k in range(nk):
            PE.wait(x.tok[k0 + k])
            a = (wh[:, k, c:c + 128], wl[:, k, c:c + 128])
            f = mm3(out, a, (x.hi[:, k0 + k, 0:n], x.lo[:, k0 + k, 0:n]), k == 0, k == nk - 1)
            if k < nk - 1:
                PE.plain(f)
        tok = PE.do(f)
        spent(i, tok)
        return tok

    def split(x, k, src, tok, scale=None, n=S):
        hi, lo = x.hi[:, k, 0:n], x.lo[:, k, 0:n]
        AC.wait(tok, *x.free[k])
        V.wait(tok, *x.free[k])
        if scale is None:
            h = AC.do(lambda e: e.copy(hi, src))
            V.wait(h)
            x.tok[k] = V.do(lambda e: e.tensor_tensor(lo, src, hi.bitcast(F), ALU.subtract))
        else:
            h = AC.do(lambda e: e.activation(hi, src, ACT.Copy, scale=scale))
            V.wait(h)
            x.tok[k] = V.do(lambda e: e.scalar_tensor_tensor(lo, src, scale, hi.bitcast(F), ALU.mult,
                                                             ALU.subtract))
        x.free[k] = []
        return x.tok[k]

    ph = Phase(PH0, "p0")
    xt = ph.sb("xt", [128, 4, D])
    d_par = dsem("d_par")
    xv = A["x"][0].rearrange("(i p) d -> p i d", p=128)
    xtoks = []
    for n in range(4):
        q = (AC, SP)[n % 2]
        xtoks.append(q.dma(dsem(f"d_x{n}"), lambda e, n=n: e.dma_start(xt[:, n, :], xv[:, n, :])))
        if n == 0:
            t_id = AC.dma(dsem("d_id"), lambda e: e.dma_start(cst[:, 0:128], const_d[:, 0:128]))
    AC.dma(d_par, lambda e: e.dma_start(cst[:, 128:], const_d[:, 128:CONST["P"][0]]))
    t_par = AC.dma(d_par, lambda e: e.dma_start(cols[:, :], cols_d))
    for i in range(NR):
        issue(i)
    htok = [None] * 8
    hread = [[] for _ in range(8)]

    for k in range(8):
        b = psr.next()
        t = b.take(PE)
        PE.wait(t_id, *xtoks)
        for i in range(4):
            f = lambda e, i=i, k=k, t=t: e.transpose(t[:, 128 * i:128 * i + 128],
                                                     xt[:, i, 128 * k:128 * k + 128], con("I"))
            if i < 3:
                PE.plain(f)
        tk = PE.do(f)
        V.wait(tk)
        htok[k] = V.do(lambda e, k=k, t=t: e.tensor_copy(H[:, k, :], t[:, :]))
        b.free = [htok[k]]

    V.wait(t_par)
    V.plain(lambda e: e.memset(small[:, 0:1], 1e-6))
    V.plain(lambda e: e.memset(small[:, 1:2], 1e-5))
    V.plain(lambda e: e.memset(small[:, 2:3], 1.0))
    V.plain(lambda e: e.tensor_copy(Ib[:, :], con("I")))
    for n, name in enumerate(("NEGT", "NEGC", "NEGS", "NEGM")):
        V.plain(lambda e, n=n, name=name: e.tensor_copy(maskb[:, n, :], con(name)))
    V.plain(lambda e: e.tensor_copy(trir[:, 0, :], con("TRI")))
    t_const = V.do(lambda e: e.tensor_copy(trir[:, 1, :], con("NONES")))
    for q in (PE, AC, PL):
        q.wait(t_const)
        q.wait(t_par)
    V.wait(t_const)
    EPS = {1e-6: small[:, 0:1], 1e-5: small[:, 1:2]}
    ONE1 = small[:, 2:3]

    norms = [0]

    class Norm:

        def __init__(self, eps, nk=8, want=True):
            self.eps, self.nk, self.k = eps, nk, 0
            self.at = norms[0]
            norms[0] += 8
            self.std = nrms[:, self.at:self.at + 4]
            self.inv = nrms[:, self.at + 4:self.at + 8]
            self.bank = None
            self.sq = []

        def square(self, src, tok):
            b = sqr.next()
            t = b.take(PL)
            PL.wait(tok)
            s = PL.do(lambda e: e.tensor_tensor(t[:, :], src, src, ALU.mult))
            self.sq.append((b, s))
            return s

        def sum_step(self):
            if self.bank is None:
                self.bank = NB
                self.bank.take(PE)
            b, s = self.sq[self.k]
            PE.wait(s)
            for i in range(4):
                f = mm(self.bank.t[:, i:i + 1], b.t[:, 128 * i:128 * i + 128], con("ONES", b=1),
                       self.k == 0 and i == 0, self.k == self.nk - 1)
                if i < 3:
                    PE.plain(f)
            self.last = PE.do(f)
            b.free = [self.last]
            self.k += 1

        def token(self):
            AC.wait(self.last)
            a = AC.do(lambda e: e.activation(self.std, self.bank.t[:, 0:4], ACT.Sqrt, bias=EPS[self.eps],
                                             scale=1.0 / 1024))
            NB.free = [a]
            V.wait(a)
            self.rtok = V.do(lambda e: e.reciprocal(self.inv, self.std))

        def finish(self, diag):
            self.token()
            self.tok = spread(self.inv, self.rtok, diag)

    def spread(inv, tok, diag):
        t = NB.take(PE)
        diag.take(V)
        V.wait(tok)
        for i in range(4):
            g = V.do(lambda e, i=i: e.tensor_scalar(diag.t[:, 128 * i:128 * i + 128], con("I"),
                                                    inv[:, i:i + 1], None, ALU.mult))
        PE.wait(g)
        for i in range(4):
            f = mm(t[:, 128 * i:128 * i + 128], con("ONES"), diag.t[:, 128 * i:128 * i + 128], True, True)
            if i < 3:
                PE.plain(f)
        m = PE.do(f)
        diag.free = [m]
        AC.wait(m, *rs.free)
        k = AC.do(lambda e: e.copy(rs.t[:, :], t[:, :]))
        NB.free = [k]
        return k

    def normed(norm, gain, goff=0, x=X):
        def f(k):
            hread[k] = [norm.square(H[:, k, :], htok[k])]
            hread[k].append(split(x, k, H[:, k, :], htok[k], col(gain, goff + k)))
            while norm.k < len(norm.sq) - 1:
                norm.sum_step()
        return f

    class Runner:

        def __init__(self, norm=None):
            self.norm, self.n, self.pend, self.late = norm, 0, [], []

        def push(self, f, g):
            b = psr.next()
            self.pend.append((g, b, f(b)))
            self.n += 1
            if self.norm is not None and self.n == 1:
                while self.norm.k < self.norm.nk:
                    self.norm.sum_step()
            if self.norm is not None and self.n == 2:
                self.norm.finish(tmp.next())
                self.norm = None
            if self.norm is None:
                self.drain(1)
            self.later(2)

        def drain(self, keep=0):
            while len(self.pend) > keep:
                g, b, t = self.pend.pop(0)
                r = g(b, t)
                if r is not None:
                    self.late.append((self.n, r))

        def later(self, lag):
            while self.late and self.late[0][0] + lag <= self.n:
                self.late.pop(0)[1]()

        def flush(self):
            self.drain()
            self.later(-1000)

    def add_h(o, src, tok, *more):
        V.wait(tok, htok[o], *hread[o], *more)
        htok[o] = V.do(lambda e: e.tensor_tensor(H[:, o, :], H[:, o, :], src, ALU.add))
        hread[o] = []
        return htok[o]

    def add_scaled(o, bank, tok, norm):
        b = tmp.next()
        t = b.take(V)
        k = scaled(bank, tok, t[:, :], norm)
        b.free = [add_h(o, t[:, :], k)]

    def scaled(bank, tok, dst, norm, p=128):
        V.wait(tok, norm.tok)
        t = V.do(lambda e: e.tensor_tensor(dst, bank.t[0:p, :], rs.t[0:p, :], ALU.mult))
        bank.free = [t]
        rs.free = [t]
        return t

    def release(x):
        x.free = [[PE.now()] for _ in x.free]

    def fence():
        t = [q.now() for q in (PE, V, AC, PL)]
        for q in (V, AC, PL, SP):
            q.wait(*t)

    def transposes(dst, blocks, toks):
        t = dst.take(PE)
        PE.wait(*toks)
        for n, (o, p, src, ident) in enumerate(blocks):
            f = lambda e, o=o, p=p, src=src, ident=ident: e.transpose(t[0:p, o:o + src.shape[0]], src, ident)
            if n < len(blocks) - 1:
                PE.plain(f)
        return PE.do(f)

    sm = Ring([Buf(sb_small[:, 16 * i:16 * i + 16]) for i in range(4)])
    XB = Pair(*(Phase(PH0 + 4 * 8 * S * i, f"xb{i}").sb("x", [128, 8, S], R) for i in range(2)), 8)

    def mixer(after):
        n1 = Norm(1e-6)
        f = normed(n1, "mix_norm")
        for k in range(8):
            f(k)
        ph = Phase(PH0, "mx")
        r1 = ph.at
        dp = Pair(ph.sb("dh", [128, 8, S], R), ph.sb("dl", [128, 8, S], R), 8)
        ph1 = Phase(r1, "my")
        xsf = ph1.sb("xsf", [128, 8, S])
        r1b = ph1.at
        xc = ph1.sb("xc", [128, 4, D])
        bc = ph.sb("bc", [128, 4, S])
        btok = ph.sb("btok", [128, 4, 2, 128])
        cb = ph.sb("cb", [128, 2, S])
        r2 = ph.at
        yp = Pair(ph.sb("yh", [128, 4, S], R), ph.sb("yl", [128, 4, S], R), 4)
        prev = Phase(r2, "mz").sb("prev", [128, 3, D])
        z = ph.sb("z", [128, 8, S])
        pads = Ring([Buf(ph.sb(f"pad{i}", [128, 528])) for i in range(2)])
        dtt = ph.sb("dtt", [128, 10, 64])
        t_pad = None
        for b in pads.bufs:
            t_pad = V.do(lambda e, b=b: e.memset(b.t[:, 0:16], 0.0))
        V.wait(t_pad)
        PL.wait(t_pad)
        ss = [Buf(ph.sb(f"ps{i}", [128, 528])) for i in range(2)]
        R1 = Runner(n1)

        def v_leave(k):
            def g(bank, tok):
                w = 2 << (k // 2)
                u = pads.next()
                t = u.take(V)
                a = scaled(bank, tok, t[:, 16:528], n1)
                src, cur, step = t, a, 1
                for n in range(k // 2 + 1):
                    d = ss[n % 2]
                    dt_ = d.take(PL)
                    PL.wait(cur)
                    lo = 2 * step - 1
                    cur = PL.do(lambda e, s_=src, d_=dt_, lo=lo, step=step: e.tensor_tensor(
                        d_[:, lo:528], s_[:, lo:528], s_[:, lo - step:528 - step], ALU.add))
                    src, step, last = dt_, 2 * step, d
                    if n:
                        ss[(n - 1) % 2].free = [cur]
                V.wait(cur)
                at = CONST["CNT"][0] + 16 * (k // 2)
                c = V.do(lambda e: e.tensor_tensor(src[:, 16:16 + w], src[:, 16:16 + w],
                                                   cst[:, at:at + w], ALU.mult))
                V.wait(c)
                b = tmp.next()
                o = b.take(V)
                c = V.do(lambda e: e.scalar_tensor_tensor(o[:, :], src[:, 16:528], 1.0 / w, t[:, 16:528],
                                                          ALU.mult, ALU.subtract))
                last.free = [c]
                u.free = [c]
                b.free = [split(dp, k, o[:, :], c)]
            return g

        for k in range(8):
            R1.push(lambda b, k=k: project(f"v{k}", X, b), v_leave(k))

        def tcol(i, p=128):
            return dtt[0:p, i, :]

        st = {}

        def dt_leave(bank, tok):
            b = tmp.next()
            t = b.take(V)
            a = scaled(bank, tok, t[0:16, :], n1, p=16)

            def late():
                o = psr.next()
                k = transposes(o, [(16 * i, 128, t[0:16, 128 * i:128 * i + 128], con("I", 0, 16, 0, 16))
                                   for i in range(4)], [a])
                b.free = [k]
                V.wait(k)
                v = lambda i: dtt[:, i, :].rearrange("p (c h) -> p c h", c=4)
                bias = col("dt_bias", 0, 16).unsqueeze(1).to_broadcast([128, 4, 16])
                k = V.do(lambda e: e.tensor_tensor(v(4), o.t[:, 0:64].rearrange("p (c h) -> p c h", c=4),
                                                   bias, ALU.add))
                o.free = [k]
                V.wait(k)
                AC.wait(k)
                AC.wait(AC.do(lambda e: e.activation(tcol(5), tcol(4), ACT.Abs)))
                k = AC.do(lambda e: e.activation(tcol(5), tcol(5), ACT.Exp, scale=-1.0))
                ka = AC.do(lambda e: e.activation(tcol(8)[:, 0:16], col("a_log", 0, 16), ACT.Exp))
                V.wait(k)

                def step(f):
                    V.wait(V.do(f))
                step(lambda e: e.tensor_scalar(tcol(6), tcol(5), 2.0, None, ALU.add))
                step(lambda e: e.reciprocal(tcol(6), tcol(6)))
                step(lambda e: e.tensor_tensor(tcol(5), tcol(5), tcol(6), ALU.mult))
                step(lambda e: e.tensor_tensor(tcol(6), tcol(5), tcol(5), ALU.mult))
                step(lambda e: e.tensor_scalar(tcol(7), tcol(6), 2.0 / 15, 2.0 / 13, ALU.mult, ALU.add))
                for n in (11, 9, 7, 5, 3, 1):
                    step(lambda e: e.tensor_tensor(tcol(7), tcol(7), tcol(6), ALU.mult))
                    step(lambda e, n=n: e.tensor_scalar(tcol(7), tcol(7), 2.0 / n, None, ALU.add))
                step(lambda e: e.tensor_tensor(tcol(7), tcol(7), tcol(5), ALU.mult))
                step(lambda e: e.scalar_tensor_tensor(tcol(0), tcol(4), 0.0, tcol(7), ALU.max, ALU.add))
                V.wait(ka)
                av = dtt[:, 8, 0:16].unsqueeze(1).to_broadcast([128, 4, 16])
                k = V.do(lambda e: e.scalar_tensor_tensor(v(1), v(0), -1.0, av, ALU.mult, ALU.mult))
                o2 = psr.next()
                t2 = o2.take(PE)
                PE.wait(k)
                k = PE.do(mm(t2[:, 0:64], con("TU"), tcol(1), True, True))
                V.wait(k)
                AC.wait(k)
                k = V.do(lambda e: e.tensor_copy(tcol(2), t2[:, 0:64]))
                V.wait(k)
                st["neg"] = V.do(lambda e: e.tensor_scalar(tcol(3), tcol(2), -1.0, None, ALU.mult))
                PE.wait(k)
                k = PE.do(mm(t2[:, 64:128], con("LAST"), tcol(2), True, True))
                AC.wait(k)
                ed = AC.do(lambda e: e.activation(tcol(9), t2[:, 64:128], ACT.Exp))
                V.wait(k, ed)
                k = V.do(lambda e: e.tensor_tensor(tcol(6), t2[:, 64:128], tcol(2), ALU.subtract))
                AC.wait(k)
                k2 = AC.do(lambda e: e.activation(tcol(6), tcol(6), ACT.Exp))
                o2.free = [ed, k]
                st["dt"], st["decay"], st["ed"] = k, k2, ed
            return late

        R1.push(lambda b: project("dt", X, b), dt_leave)

        def conv_leave(k, dst, nxt=None):
            def g(bank, tok):
                u = pads.next()
                t = u.take(V)
                a = scaled(bank, tok, t[:, 16:528], n1)
                b = tmp.next()
                o = b.take(AC)
                AC.wait(a, t_pad)
                w = lambda j: col("conv_w", 12 * j + k)
                c = AC.do(lambda e: e.activation(o[:, :], t[:, 13:525], ACT.Copy, scale=w(0)))
                for j in range(1, 4):
                    V.wait(c)
                    c = V.do(lambda e, j=j: e.scalar_tensor_tensor(
                        o[:, :], t[:, 13 + j:525 + j], w(j), o[:, :], ALU.mult, ALU.add))
                u.free = [c]
                AC.wait(c)
                s_ = AC.do(lambda e: e.activation(dst, o[:, :], ACT.Silu, bias=col("conv_b", k)))
                b.free = [s_]
                if nxt is None:
                    return None
                return lambda: nxt(s_)
            return g

        btk = {}

        def b_next(g):
            def f(s_):
                o = psr.next()
                k = transposes(o, [(128 * c, 128, bc[:, g, 128 * c:128 * c + 128], con("I"))
                                   for c in range(4)], [s_])
                V.wait(k)
                btk[g] = V.do(lambda e: e.tensor_copy(
                    btok[:, :, g, :], o.t[:, :].rearrange("p (c n) -> p c n", c=4)))
                o.free = [btk[g]]
            return f

        def c_next(g):
            def f(s_):
                btk[("c", g)] = s_
                o = psr.next()
                t = o.take(PE)
                PE.wait(s_)
                for c in range(4):
                    m = mm(t[:, 128 * c:128 * c + 128], bc[:, g, 128 * c:128 * c + 128],
                           bc[:, 2 + g, 128 * c:128 * c + 128], True, True)
                    if c < 3:
                        PE.plain(m)
                k = PE.do(m)
                AC.wait(k)
                btk[("cb", g)] = AC.do(lambda e: e.copy(cb[:, g, :], t[:, :]))
                o.free = [btk[("cb", g)]]
            return f


        def pool_jobs(g, base):
            cell = {}
            for m in range(2):
                def f(b, m=m):
                    if m == 0:
                        cell["u"] = weights(f"pool{g}")
                    return project(cell["u"], dp, b, nk=2, c=128 * m, k0=2 * g)

                def leave(bank, tok, m=m):
                    k = 2 * g + m
                    bank.free = [split(yp, k - base, bank.t[:, :], tok, col("pool_scale", k))]
                R1.push(f, leave)

        def out_pool(half):
            for o in range(4):
                cell = {}
                for m in range(2):
                    def f(b, o=o, m=m, cell=cell):
                        if m == 0:
                            cell["u"] = weights(f"op{half}{o}")
                        return project(cell["u"], yp, b, nk=4, c=128 * m)

                    def leave(bank, tok, o=o, m=m):
                        bank.free = [add_h(2 * o + m, bank.t[:, :], tok)]
                    R1.push(f, leave)
            release(yp)

        pool_jobs(0, 0)
        pool_jobs(1, 0)
        nx = [b_next(0), b_next(1), c_next(0), c_next(1)]
        for k in range(8, 12):
            R1.push(lambda b, k=k: project(f"xbc{k}", X, b), conv_leave(k, bc[:, k - 8, :], nx[k - 8]))
        out_pool(0)
        pool_jobs(2, 4)
        pool_jobs(3, 4)
        release(dp)
        t_dp = PE.now()
        AC.wait(t_dp)
        V.wait(t_dp)
        xtok, xctok = {}, {}

        def xs_next(k):
            def f(s_):
                xtok[k] = s_
                o = psr.next()
                q = transposes(o, [(128 * c, 128, xsf[:, k, 128 * c:128 * c + 128], con("I"))
                                   for c in range(4)], [s_])
                V.wait(q, st["dt"])
                src = o.t[:, :].rearrange("p (c j d) -> p c j d", c=4, j=2)
                dst = xc[:, :, 128 * k:128 * k + 128].rearrange("p c (j d) -> p c j d", j=2)
                dd = dtt[:, 0, :].rearrange("p (c h) -> p c h", c=4)[:, :, 2 * k:2 * k + 2]
                xctok[k] = V.do(lambda e: e.tensor_tensor(
                    dst, src, dd.unsqueeze(3).to_broadcast([128, 4, 2, 64]), ALU.mult))
                o.free = [xctok[k]]
            return f

        for k in range(8):
            R1.push(lambda b, k=k: project(f"xbc{k}", X, b), conv_leave(k, xsf[:, k, :], xs_next(k)))
            if k == 1:
                out_pool(1)
        t_yp = PE.now()

        ztok = {}

        def z_leave(k):
            def g(bank, tok):
                b = sqr.next()
                t = b.take(V)
                a = scaled(bank, tok, t[:, :], n1)
                AC.wait(a)
                ztok[k] = AC.do(lambda e: e.activation(z[:, k, :], t[:, :], ACT.Silu))
                b.free = [ztok[k]]
            return g

        def z_job(k):
            R1.push(lambda b, k=k: project(f"z{k}", X, b), z_leave(k))
            if k == 7:
                release(X)

        z_job(0)
        z_job(1)
        z_job(2)
        R1.flush()
        V.wait(t_yp)
        ptok = {}
        dec = dtt[:, 6, :].rearrange("p (c h) -> p c h", c=4)
        edc = dtt[:, 9, :].rearrange("p (c h) -> p c h", c=4)
        PL.wait(st["decay"], *[xctok[k] for k in range(8)])
        for c in range(3):
            for g in range(2):
                b = tmp.next()
                t = b.take(PL)
                xd = PL.do(lambda e, t=t, c=c, g=g: e.tensor_tensor(
                    t[:, :].rearrange("p (h d) -> p h d", h=8),
                    xc[:, c, 512 * g:512 * g + 512].rearrange("p (h d) -> p h d", h=8),
                    dec[:, c, 8 * g:8 * g + 8].unsqueeze(2).to_broadcast([128, 8, 64]), ALU.mult))
                o = psr.next()
                bt = o.take(PE)
                PE.wait(xd, btk[g])
                k = PE.do(mm(bt[:, :], btok[:, c, g, :], t[:, :], True, True))
                b.free = [k]
                V.wait(k, st["ed"])
                dst = prev[:, c, 512 * g:512 * g + 512]
                if c == 0:
                    ptok[(c, g)] = V.do(lambda e, dst=dst, bt=bt: e.tensor_copy(dst, bt[:, :]))
                else:
                    V.wait(ptok[(c - 1, g)])
                    k = V.do(lambda e, dst=dst, c=c, g=g: e.tensor_tensor(
                        dst.rearrange("p (h d) -> p h d", h=8),
                        prev[:, c - 1, 512 * g:512 * g + 512].rearrange("p (h d) -> p h d", h=8),
                        edc[:, c, 8 * g:8 * g + 8].unsqueeze(2).to_broadcast([128, 8, 64]), ALU.mult))
                    V.wait(k)
                    ptok[(c, g)] = V.do(lambda e, dst=dst, bt=bt: e.tensor_tensor(dst, dst, bt[:, :], ALU.add))
                o.free = [ptok[(c, g)]]
                if c == 0 and g == 0:
                    z_job(3)

        n2 = Norm(1e-6)
        YP = Pair(Phase(r1b, "yp").sb("hi", [128, 8, S], R), None, 8)
        YP.lo = Phase(r2, "yq").sb("lo", [128, 8, S], R)
        adt = dtt[:, 1, :].rearrange("p (c h) -> p c h", c=4)
        nacs = dtt[:, 3, :].rearrange("p (c h) -> p c h", c=4)
        heads = {}

        def head_a(h):
            g = h // 8
            o = psr.next()
            t = o.take(PE)
            PE.wait(st["dt"])
            for c in range(4):
                m = mm(t[:, 128 * c:128 * c + 128], adt[:, c, h:h + 1].to_broadcast([128, 128]),
                       con("TU"), c == 0, False)
                if c < 3:
                    PE.plain(m)
            k = PE.do(m)
            eb, sg = tmp.next(), tmp.next()
            et, sgt = eb.take(AC), sg.take(AC)
            AC.wait(k, st["neg"])
            a = AC.do(lambda e: e.activation(et[:, :], t[:, :], ACT.Exp))
            PE.wait(a)
            for c in range(4):
                m = mm(t[:, 128 * c:128 * c + 128], Ib[:, :], maskb[:, 0, :], False, c == 3)
                if c < 3:
                    PE.plain(m)
            k = PE.do(m)
            AC.wait(k)
            for c in range(4):
                s_ = AC.do(lambda e, c=c: e.activation(sgt[:, 128 * c:128 * c + 128],
                                                       t[:, 128 * c:128 * c + 128], ACT.Exp,
                                                       bias=nacs[:, c, h:h + 1]))
            o.free = [s_]
            PL.wait(a, btk[("c", g)])
            ce = PL.do(lambda e: e.tensor_tensor(et[:, :], bc[:, 2 + g, :], et[:, :], ALU.mult))
            V.wait(s_, btk[("cb", g)])
            m_ = V.do(lambda e: e.tensor_tensor(sgt[:, :], sgt[:, :], cb[:, g, :], ALU.mult))
            heads[h] = (eb, sg, ce, m_)

        ybank = {}

        def head_b(h):
            eb, sg, ce, m_ = heads.pop(h)
            g, p0 = h // 8, 64 * (h % 2)
            if h % 2 == 0:
                ybank[h // 2] = PS[6 + (h // 2) % 2]
                ybank[h // 2].take(PE)
            o = ybank[h // 2]
            PE.wait(ce, m_, xctok[h // 2], ptok[(2, g)])
            for c in range(4):
                out = o.t[p0:p0 + 64, 128 * c:128 * c + 128]
                PE.plain(mm(out, xc[:, c, 64 * h:64 * h + 64], sg.t[:, 128 * c:128 * c + 128],
                            c == 0, c == 0))
                if c:
                    m = mm(out, prev[:, c - 1, 64 * h:64 * h + 64], eb.t[:, 128 * c:128 * c + 128],
                           False, True)
                    if c < 3:
                        PE.plain(m)
            k = PE.do(m)
            eb.free = [k]
            sg.free = [k]
            if h % 2:
                j = h // 2
                V.wait(k, xtok[j])
                k = V.do(lambda e: e.scalar_tensor_tensor(xsf[:, j, :], xsf[:, j, :], col("d_skip", j),
                                                          o.t[:, :], ALU.mult, ALU.add))
                o.free = [k]
                V.wait(k, ztok[j])
                ytok[j] = V.do(lambda e: e.tensor_tensor(xsf[:, j, :], xsf[:, j, :], z[:, j, :], ALU.mult))

        ytok = {}
        R1.flush()
        psr.bufs, saved = PS[0:6], psr.bufs
        for h in range(16):
            if h < 4:
                z_job(4 + h)
            elif h == 4:
                R1.flush()
            head_a(h)
            if h >= 1:
                head_b(h - 1)
        R1.flush()
        head_b(15)
        psr.bufs = saved
        AC.wait(PE.now())
        V.wait(PE.now())
        for k in range(8):
            n2.square(xsf[:, k, :], ytok[k])
            split(YP, k, xsf[:, k, :], ytok[k], col("ssd_norm", k))
            if k:
                n2.sum_step()
        R2 = Runner(n2)
        for o in range(8):
            def leave(bank, tok, o=o):
                add_scaled(o, bank, tok, n2)
                after(o)
            R2.push(lambda b, o=o: project(f"os{o}", YP, b), leave)
        R2.flush()

    def token_major(units, x, norm, dst, width, nt, k2, scale=None):
        banks = [psr.next() for _ in range(nt)]
        for b in banks:
            b.take(PE)
        k = 0
        for n, name in enumerate(units):
            i, wh, wl = weights(name)
            for kk in range(k2):
                PE.wait(x.tok[k])
                for t in range(nt):
                    a = (x.hi[:, k, 128 * t:128 * t + 128], x.lo[:, k, 128 * t:128 * t + 128])
                    last = n == len(units) - 1 and kk == k2 - 1
                    f = mm3(banks[t].t[:, 0:width], a, (wh[:, kk, :], wl[:, kk, :]), k == 0, last)
                    if not last and (t < nt - 1 or kk < k2 - 1):
                        PE.plain(f)
                    else:
                        tok = PE.do(f)
                        if last:
                            banks[t].done = tok
                k += 1
            spent(i, tok)
        out = None
        for t in range(nt):
            AC.wait(banks[t].done)
            if scale is None:
                out = AC.do(lambda e, t=t: e.copy(dst(t), banks[t].t[:, 0:width]))
            else:
                AC.wait(norm.rtok)
                out = AC.do(lambda e, t=t: e.activation(dst(t), banks[t].t[:, 0:width], ACT.Copy,
                                                        scale=scale[:, t:t + 1]))
            banks[t].free = [out]
        return out

    def xattn(n3, after):
        fence()
        ph = Phase(PH0, "xa")
        OP = Pair(ph.sb("oh", [128, 8, S], R), ph.sb("ol", [128, 8, S], R), 8)
        mp = Pair(ph.sb("mh", [128, 8, ML], R), ph.sb("ml", [128, 8, ML], R), 8)
        kT = ph.sb("kT", [128, 8, ML])
        vt = ph.sb("vt", [128, 2, D])
        r = ph.at
        q = ph.sb("q", [128, 8, S])
        mt = Phase(r, "xb").sb("mt", [128, 2, D])
        pts = Ring([Buf(ph.sb("pt0", [128, 2, S]))])
        mst = ph.sb("mst", [128, 8])
        d_mem = dsem("d_mem")
        t = SP.dma(d_mem, lambda e: e.dma_start(mt[:, :, :], A["mem"][0].rearrange("(i p) d -> p i d", p=128)))
        scr = tmp.next()
        scr.take(AC)
        AC.wait(t)
        for i in range(2):
            for j in range(2):
                a = AC.do(lambda e, i=i, j=j: e.activation(scr.t[:, :], mt[:, i, 512 * j:512 * j + 512],
                                                           ACT.Square, accum_out=mst[:, 2 * i + j:2 * i + j + 1]))
                AC.wait(a)
        V.wait(a)
        m2 = mst[:, 0:4].rearrange("p (i j) -> p i j", j=2)
        b = V.do(lambda e: e.tensor_tensor(mst[:, 4:6], m2[:, :, 0], m2[:, :, 1], ALU.add))
        AC.wait(b)
        a = AC.do(lambda e: e.activation(mst[:, 4:6], mst[:, 4:6], ACT.Sqrt, bias=EPS[1e-6], scale=1.0 / 1024))
        scr.free = [a]
        V.wait(a)
        b = V.do(lambda e: e.reciprocal(mst[:, 6:8], mst[:, 4:6]))
        V.wait(b)
        for i in range(2):
            b = V.do(lambda e, i=i: e.tensor_scalar(mt[:, i, :], mt[:, i, :], mst[:, 6 + i:7 + i], None, ALU.mult))
        for k in range(8):
            o = psr.next()
            tk = transposes(o, [(128 * i, 128, mt[:, i, 128 * k:128 * k + 128], con("I")) for i in range(2)], [b])
            o.free = [split(mp, k, o.t[:, 0:ML], tk, col("mem_norm", k), n=ML)]
        tmt = PE.now()
        Rk = Runner()
        kt = {}
        for o in range(8):
            def leave(bank, tok, o=o):
                V.wait(tok)
                kt[o] = V.do(lambda e: e.tensor_copy(kT[:, o, :], bank.t[:, 0:ML]))
                bank.free = [kt[o]]
            Rk.push(lambda b, o=o: project(f"mk{o}", mp, b, n=ML), leave)
        Rk.flush()
        for blk in range(2):
            tv = token_major([f"mv{blk}{kk}" for kk in range(4)], mp, None,
                             lambda t, blk=blk: vt[:, t, 512 * blk:512 * blk + 512], 512, 2, 2)
        V.wait(tmt)
        Rq = Runner(n3)
        qt = {}
        for o in range(8):
            def leave(bank, tok, o=o):
                qt[o] = scaled(bank, tok, q[:, o, :], n3)
            Rq.push(lambda b, o=o: project(f"xq{o}", X, b), leave)
        release(X)
        Rq.flush()
        steps = [(h, i) for h in range(4) for i in range(4)]
        live, ptc = {}, {}
        sc = 1.0 / 16

        def sa(n):
            h, i = steps[n]
            o = psr.next()
            t = o.take(PE)
            PE.wait(qt[2 * h + 1], kt[7])
            for kk in range(2):
                f = mm(t[:, 0:ML], q[:, 2 * h + kk, 128 * i:128 * i + 128], kT[:, 2 * h + kk, :], kk == 0, kk == 1)
                if kk == 0:
                    PE.plain(f)
            k = PE.do(f)
            c = sm.next()
            w = c.take(V)
            V.wait(k)
            k = V.do(lambda e: e.reduce_max(w[:, 0:1], t[:, 0:ML], AX.X))
            V.wait(k)
            k = V.do(lambda e: e.tensor_scalar(w[:, 1:2], w[:, 0:1], -sc, None, ALU.mult))
            p = tmp.next()
            pt = p.take(AC)
            AC.wait(k)
            k = AC.do(lambda e: e.activation(pt[:, 0:ML], t[:, 0:ML], ACT.Exp, bias=w[:, 1:2], scale=sc,
                                             accum_out=w[:, 2:3]))
            o.free = [k]
            V.wait(k)
            k = V.do(lambda e: e.reciprocal(w[:, 3:4], w[:, 2:3]))
            V.wait(k)
            k = V.do(lambda e: e.tensor_scalar(pt[:, 0:ML], pt[:, 0:ML], w[:, 3:4], None, ALU.mult))
            c.free = [k]
            live[n] = (p, k)

        def sb_(n):
            h, i = steps[n]
            p, k = live.pop(n)
            o = psr.next()
            k = transposes(o, [(128 * j, 128, p.t[:, 128 * j:128 * j + 128], con("I")) for j in range(2)], [k])
            p.free = [k]
            if i == 0:
                ptc["b"] = pts.next()
                ptc["b"].take(V)
            P_ = ptc["b"]
            V.wait(k)
            k = V.do(lambda e, o=o: e.tensor_copy(P_.t[:, :, 128 * i:128 * i + 128],
                                             o.t[:, 0:256].rearrange("p (j t) -> p j t", j=2)))
            o.free = [k]
            if i == 3:
                PE.wait(k, tv)
                for m in range(2):
                    o = psr.next()
                    t = o.take(PE)
                    cc = 2 * h + m
                    PE.plain(mm(t[:, :], vt[:, 0, 128 * cc:128 * cc + 128], P_.t[:, 0, :], True, False))
                    kk = PE.do(mm(t[:, :], vt[:, 1, 128 * cc:128 * cc + 128], P_.t[:, 1, :], False, True))
                    o.free = [split(OP, cc, t[:, :], kk)]
                P_.free = [kk]

        for n in range(16):
            sa(n)
            if n >= 2:
                sb_(n - 2)
        sb_(14)
        sb_(15)
        Ro = Runner()
        for o in range(8):
            def leave(bank, tok, o=o):
                bank.free = [add_h(o, bank.t[:, :], tok)]
                after(o)
            Ro.push(lambda b, o=o: project(f"xo{o}", OP, b), leave)
        Ro.flush()

    def ffn(tag, groups, x, norm, at, after, gated):
        fence()
        ph = Phase(at, f"f{tag}")
        hid = [Pair(ph.sb(f"h{i}", [128, 4, S], R), ph.sb(f"l{i}", [128, 4, S], R), 4) for i in range(2)]
        Rf = Runner(norm)
        sil, cell = {}, {}

        def gate_leave(c):
            def g(bank, tok):
                b = tmp.next()
                t = b.take(V)
                k = scaled(bank, tok, t[:, :], norm)
                AC.wait(k)
                sil[c] = (b, AC.do(lambda e: e.activation(t[:, :], t[:, :], ACT.Silu)))
            return g

        def up_leave(c, pair, k_):
            def g(bank, tok):
                b = tmp.next()
                t = b.take(V)
                k = scaled(bank, tok, t[:, :], norm)
                b2, s_ = sil.pop(c)
                V.wait(k, s_)
                k = V.do(lambda e: e.tensor_tensor(t[:, :], t[:, :], b2.t[:, :], ALU.mult))
                b2.free = [k]
                b.free = [split(pair, k_, t[:, :], k)]
            return g

        def relu_leave(c, pair, k_):
            def g(bank, tok):
                b = tmp.next()
                t = b.take(V)
                k = scaled(bank, tok, t[:, :], norm)
                V.wait(k)
                k = V.do(lambda e: e.scalar_tensor_tensor(t[:, :], t[:, :], 0.0, t[:, :], ALU.max, ALU.mult))
                b.free = [split(pair, k_, t[:, :], k)]
            return g

        for kind, g in ffn_order(groups):
            pair, c0 = hid[g % 2], sum(groups[:g])
            if kind == "up":
                for c in range(c0, c0 + groups[g]):
                    if gated:
                        Rf.push(lambda b, c=c: project(f"{tag}g{c}", x, b), gate_leave(c))
                        Rf.push(lambda b, c=c: project(f"{tag}u{c}", x, b), up_leave(c, pair, c - c0))
                    else:
                        Rf.push(lambda b, c=c: project(f"{tag}u{c}", x, b), relu_leave(c, pair, c - c0))
                if g == len(groups) - 1:
                    release(x)
            else:
                n = groups[g]
                for o in range(8):
                    def f(b, o=o):
                        per = 8 // n
                        if o % per == 0:
                            cell["u"] = weights(f"{tag}d{g}_{o // per}")
                        return project(cell["u"], pair, b, nk=n, c=128 * (o % per))

                    def leave(bank, tok, o=o, g=g):
                        bank.free = [add_h(o, bank.t[:, :], tok)]
                        if g == len(groups) - 1:
                            after(o)
                    Rf.push(f, leave)
                release(pair)
        Rf.flush()

    def stick(x, norm, OPx, after):
        fence()
        ph = Phase(PH0, "st")
        q = ph.sb("q", [128, 8, S])
        kk_ = ph.sb("k", [128, 8, S])
        vt = ph.sb("v", [128, 4, D])
        OFF = [0, 512, 1024, 896]
        BK = [0, 1, 2, 1]
        wd = [512 - 128 * j for j in range(4)]
        W = [512, 512, 256]

        def sl(n):
            return slice(512 * n, 512 * n + W[n])

        Lp = Ring([Buf(ph.sb(f"L{i}", [128, 1280])) for i in range(3)])
        Ab = Ring([Buf(ph.sb(f"A{i}", [128, 1280])) for i in range(1)])
        Lh = Ring([Buf(ph.sb(f"Lh{i}", [128, 1280], R)) for i in range(2)])
        Ll = Ring([Buf(ph.sb(f"Ll{i}", [128, 1280], R)) for i in range(2)])
        Rq = Runner(norm)
        qt = {}
        for o in range(16):
            def leave(bank, tok, o=o):
                V.wait(tok, norm.tok)
                if o < 8:
                    qt[o] = V.do(lambda e: e.scalar_tensor_tensor(q[:, o, :], bank.t[:, :], 0.125, rs.t[:, :],
                                                                  ALU.mult, ALU.mult))
                    bank.free = [qt[o]]
                    rs.free = [qt[o]]
                else:
                    qt[o] = scaled(bank, tok, kk_[:, o - 8, :], norm)
            Rq.push(lambda b, o=o: project(f"sq{o}", x, b), leave)
        Rq.flush()
        for blk in range(2):
            tv = token_major([f"sv{blk}{c}" for c in range(4)], x, norm,
                             lambda t, blk=blk: vt[:, t, 512 * blk:512 * blk + 512], 512, 4, 2, norm.inv)
        release(x)
        psr.bufs, saved = PS[0:6], psr.bufs
        AC.plain(lambda e: e.preload_act_table_set("natural_log_exp_and_others"))
        live = {}
        ob = {}

        def a_(h):
            p0 = 64 * (h % 2)
            c = h // 2
            bk = [psr.next() for _ in range(3)]
            for b in bk:
                b.take(PE)
            PE.wait(qt[c], qt[8 + c])
            for j in (0, 1, 2, 3):
                t = bk[BK[j]].t[:, OFF[j] % 512:OFF[j] % 512 + wd[j]]
                f = mm(t, kk_[p0:p0 + 64, c, 128 * j:128 * j + 128], q[p0:p0 + 64, c, 128 * j:512],
                       j != 3, False)
                if j < 3:
                    PE.plain(f)
            k = PE.do(f)
            L, Abf = Lp.next(), Ab.next()
            l, a = L.take(V), Abf.take(V, AC)
            V.wait(k)
            AC.wait(k)
            V.wait(V.do(lambda e: e.tensor_scalar(l[:, 0:512], bk[0].t[:, :], 0.0, None, ALU.max)))
            d = V.do(lambda e: e.scalar_tensor_tensor(a[:, 0:512], l[:, 0:512], 2.0, bk[0].t[:, :], ALU.mult,
                                                      ALU.subtract))
            ln = {}
            for n in (1, 2):
                k = AC.do(lambda e, n=n: e.activation(a[:, sl(n)], bk[n].t[:, 0:W[n]], ACT.Abs))
            AC.wait(k)
            k = AC.do(lambda e: e.activation(a[:, 512:1280], a[:, 512:1280], ACT.Exp, scale=-1.0))
            AC.wait(k)
            ln[1] = ln[2] = AC.do(lambda e: e.activation(a[:, 512:1280], a[:, 512:1280], ACT.Ln, bias=ONE1))
            live[h] = (bk, L, Abf, ln, d)

        def a3_(h):
            bk, L, Abf, ln, d = live[h]
            a = Abf.t
            AC.wait(d)
            k = AC.do(lambda e: e.activation(a[:, 0:512], a[:, 0:512], ACT.Exp, scale=-1.0))
            AC.wait(k)
            ln[0] = AC.do(lambda e: e.activation(a[:, 0:512], a[:, 0:512], ACT.Ln, bias=ONE1))

        def b_(h):
            bk, L, hb, lb, k = live[h]
            for j in (3, 2, 1, 0):
                t = bk[BK[j]].t
                o = OFF[j] % 512
                PE.wait(k[BK[j]])
                if j == 1:
                    PE.wait(k[2])
                PE.plain(mm(t[:, o:o + 128], Ib[:, :], maskb[:, 2, :], False, False))
                for i in range(j, 4):
                    out = t[:, o + 128 * (i - j):o + wd[j]]
                    for part in (hb.t, lb.t):
                        f = mm(out, trir[:, 0 if i == j else 1, :], part[:, OFF[i]:OFF[i] + wd[i]], False,
                               i == 3 and part is lb.t)
                        if not (i == 3 and part is lb.t):
                            PE.plain(f)
                d = PE.do(f)
                if j != 3:
                    n = BK[j]
                    AC.wait(d)
                    w_ = AC.do(lambda e, n=n: e.activation(L.t[:, sl(n)], bk[n].t[:, 0:W[n]], ACT.Exp))
                    bk[n].free = [w_]
            hb.free = [d]
            lb.free = [d]
            live[h] = (L, w_)

        def a2_(h):
            bk, L, Abf, ln, _ = live[h]
            l, a = L.t, Abf.t
            hb, lb = Lh.next(), Ll.next()
            hi, lo = hb.take(PL), lb.take(V)
            k = {}
            hd = {}

            def low(n):
                V.wait(hd[n])
                k[n] = V.do(lambda e: e.tensor_tensor(lo[:, sl(n)], l[:, sl(n)], hi[:, sl(n)].bitcast(F),
                                                      ALU.subtract))

            for n in (1, 2, 0):
                V.wait(ln[n])
                if n:
                    d = V.do(lambda e, n=n: e.scalar_tensor_tensor(l[:, sl(n)], bk[n].t[:, 0:W[n]], 0.0,
                                                                   a[:, sl(n)], ALU.max, ALU.add))
                else:
                    d = V.do(lambda e: e.tensor_tensor(l[:, 0:512], l[:, 0:512], a[:, 0:512], ALU.add))
                V.wait(d)
                for j in range(4):
                    if BK[j] == n:
                        m = V.do(lambda e, j=j: e.tensor_tensor(l[:, OFF[j]:OFF[j] + 128],
                                                                l[:, OFF[j]:OFF[j] + 128], con("MS"), ALU.mult))
                PL.wait(m)
                hd[n] = PL.do(lambda e, n=n: e.tensor_scalar(hi[:, sl(n)], l[:, sl(n)], 1.0, 0.0, ALU.mult,
                                                             ALU.add))
                if n != 1:
                    low({2: 1, 0: 2}[n])
            low(0)
            Abf.free = [m]
            live[h] = (bk, L, hb, lb, k)

        def c_(h):
            L, d = live.pop(h)
            p0 = 64 * (h % 2)
            if h % 2 == 0:
                ob[0] = PS[6 + (h // 2) % 2]
                ob[0].take(PE)
            o = ob[0]
            PE.wait(d, tv)
            for j in range(4):
                f = mm(o.t[p0:p0 + 64, 128 * j:512], vt[:, j, 64 * h:64 * h + 64], L.t[:, OFF[j]:OFF[j] + wd[j]],
                       j == 0, j == 3)
                if j < 3:
                    PE.plain(f)
            k = PE.do(f)
            L.free = [k]
            if h % 2:
                o.free = [split(OPx, h // 2, o.t[:, :], k)]

        for h in range(16):
            if h >= 1:
                a2_(h - 1)
            a_(h)
            if h >= 1:
                b_(h - 1)
            a3_(h)
            if h >= 2:
                c_(h - 2)
        a2_(15)
        b_(15)
        c_(14)
        c_(15)
        psr.bufs = saved
        fence()
        Ro = Runner()
        for o in range(8):
            def leave(bank, tok, o=o):
                bank.free = [add_h(o, bank.t[:, :], tok)]
                after(o)
            Ro.push(lambda b, o=o: project(f"so{o}", OPx, b), leave)
        release(OPx)
        Ro.flush()

    def nsa(xkv, xq, norm, OPx, after):
        fence()
        ph = Phase(PH0 + 8 * S * 8, "ns")
        q = ph.sb("q", [128, 8, S])
        vs = [ph.sb("vs", [128, 4, 256]), ph.sb("vw", [128, 4, 256])]
        gat = ph.sb("gat", [128, 4, 48])
        kc = ph.sb("kc", [128, 4, 31])
        vc = ph.sb("vc", [31, 4, 64])
        ptc = Buf(ph.sb("ptc", [31, S]))
        r3 = ph.at
        rope = ph.sb("rope", [128, 2, S])
        w2 = ph.sb("w2", [128, 2, 2, 2, 64])
        rmat = ph.sb("rmat", [128, 5, 128])
        hdn = ph.sb("hdn", [128, 2, 2, 124])
        cm = Ring([Buf((ph.sb(f"ch{i}", [128, 124], R), ph.sb(f"cl{i}", [128, 124], R))) for i in range(3)])
        r4 = ph.at
        d_c = dsem("d_cmp")
        tw = None
        for c in range(2):
            for dup in range(2):
                tw = SP.dma(d_c, lambda e, c=c, dup=dup: e.dma_start(
                    w2[:, c, :, dup, :], A["cmp_w2_2"][c].rearrange("(k p) d -> p k d", p=128)))
        a0 = CONST["P"][0]
        tw = SP.dma(d_c, lambda e: e.dma_start(rmat[:, :, :], const_d[:, a0:a0 + 640].rearrange("p (k n) -> p k n", k=5)))
        tw = SP.dma(d_c, lambda e: e.dma_start(rope[:, :, :], const_d[:, a0 + 640:a0 + 1664].rearrange("p (k n) -> p k n", k=2)))
        RCt, RSt = rope[:, 0, :], rope[:, 1, :]
        Rq = Runner(norm)
        qt, qrt = {}, {}
        for o in range(8):
            def leave(bank, tok, o=o):
                qt[o] = scaled(bank, tok, q[:, o, :], norm)
            Rq.push(lambda b, o=o: project(f"nq{o}", xq, b), leave)
        Rq.flush()
        i, wh, wl = weights("ng")
        gb = psr.next()
        t = gb.take(PE)
        for ti in range(4):
            for k in range(8):
                a = (xq.hi[:, k, 128 * ti:128 * ti + 128], xq.lo[:, k, 128 * ti:128 * ti + 128])
                f = mm3(t[:, 48 * ti:48 * ti + 48], a, (wh[:, k, :], wl[:, k, :]), ti == 0 and k == 0, k == 7)
                if not (ti == 3 and k == 7):
                    PE.plain(f)
        k = PE.do(f)
        spent(i, k)
        V.wait(k, norm.rtok)
        for ti in range(4):
            k = V.do(lambda e, ti=ti, t=t: e.scalar_tensor_tensor(gat[:, ti, :], t[:, 48 * ti:48 * ti + 48],
                                                             norm.inv[:, ti:ti + 1], col("gate_b", 0, 48),
                                                             ALU.mult, ALU.add))
        gb.free = [k]
        AC.wait(k)
        k = AC.do(lambda e: e.activation(gat[:, :, :], gat[:, :, :], ACT.Exp, scale=-1.0))
        V.wait(k)
        k = V.do(lambda e: e.tensor_scalar(gat[:, :, :], gat[:, :, :], 1.0, None, ALU.add))
        V.wait(k)
        tg = V.do(lambda e: e.reciprocal(gat[:, :, :], gat[:, :, :]))
        fence()
        pk = Phase(PH0, "nk")
        X2 = pk.sb("x2", [128, 2, 4, 512])
        kd = [pk.sb("ks", [128, 4, S]), pk.sb("kw", [128, 4, S])]
        pts = Phase(PH0, "nt").sb("pts", [128, 2, 4, S])
        ph2 = Phase(ph.at, "nq")
        qr = ph2.sb("qr", [128, 8, S])
        PTS = Buf(pts)
        PE.wait(tw)
        V.wait(tw)
        PL.wait(tw)
        Rk = Runner()
        x2t = []
        for o in range(4):
            def leave(bank, tok, o=o):
                c, g0 = o // 2, 2 * (o % 2)
                V.wait(tok, norm.tok)
                for g in range(2):
                    s0 = 64 * g
                    k = V.do(lambda e, g=g, s0=s0: e.tensor_tensor(
                        X2[0:64, c, g0 + g, :], bank.t[s0:s0 + 64, :], rs.t[0:64, :], ALU.mult))
                    k = V.do(lambda e, g=g, s0=s0: e.tensor_tensor(
                        X2[64:128, c, g0 + g, 0:511], bank.t[s0:s0 + 64, 1:512], rs.t[0:64, 1:512], ALU.mult))
                bank.free = [k]
                rs.free = [k]
                x2t.append(k)
            Rk.push(lambda b, o=o: project(f"nc{o}", xkv, b), leave)
        kdt = {}

        def rotate(src, tok, mats, dst, rel, key):
            PE.wait(tok)
            o1 = None
            if mats[0] is not None:
                o1 = psr.next()
                PE.plain(mm(o1.take(PE)[:, :], mats[0], src, True, True))
            o2 = psr.next()
            k = PE.do(mm(o2.take(PE)[:, :], mats[1], src, True, True))
            b = sqr.next()
            bt = b.take(V)
            V.wait(k, tok)
            s1 = src if o1 is None else o1.t[:, :]
            a = V.do(lambda e: e.tensor_tensor(dst, s1, RCt, ALU.mult))
            c = V.do(lambda e: e.tensor_tensor(bt[:, :], o2.t[:, :], RSt, ALU.mult))
            if o1 is not None:
                o1.free = [a]
            o2.free = [c]
            PL.wait(a, c)
            kdt[key] = PL.do(lambda e: e.tensor_tensor(dst, dst, bt[:, :], ALU.add))
            b.free = [kdt[key]]
            return k

        for kind in range(2):
            for o in range(2):
                def leave(bank, tok, kind=kind, o=o):
                    b = tmp.next()
                    t = b.take(V)
                    a = scaled(bank, tok, t[:, :], norm)

                    def late():
                        for g in range(2):
                            k = rotate(t[:, :], a, (rmat[:, 1 + g, :], rmat[:, 3 + g, :]),
                                       kd[kind][:, 2 * o + g, :], None, ("k", kind, 2 * o + g))
                        b.free = [k]
                    return late
                Rk.push(lambda b, kind=kind, o=o: project(f"nk{kind}{o}", xkv, b), leave)
        Rk.drain()
        for kind in range(2):
            tv = token_major([f"nv{kind}{c}" for c in range(2)], xkv, norm,
                             lambda t, kind=kind: vs[kind][:, t, :], 256, 4, 4, norm.inv)
            Rk.later(-1000)
        release(xkv)
        for o in range(8):
            rotate(q[:, o, :], qt[o], (None, rmat[:, 0, :]), qr[:, o, :], None, ("q", o))
        for c in range(2):
            bk = [psr.next(), psr.next()]
            for b in bk:
                b.take(PE)
            for j in range(16):
                if j % 4 == 0:
                    i, wh, wl = weights(f"c1{c}{j // 4}")
                b = cm.next()
                hi, lo = b.take(AC, V)
                src = X2[:, c, :, 2 * j:2 * j + 481:16]
                hv, lv = (u[:, :].rearrange("p (g n) -> p g n", g=4) for u in (hi, lo))
                pos = col("cmp_pos", 16 * c + j)
                AC.wait(*x2t)
                V.wait(*x2t)
                k = AC.do(lambda e, src=src, hv=hv, pos=pos: e.activation(hv, src, ACT.Identity, bias=pos))
                V.wait(k)
                k = V.do(lambda e, src=src, hv=hv, lv=lv, pos=pos: e.scalar_tensor_tensor(
                    lv, src, pos, hv.bitcast(F), ALU.add, ALU.subtract))
                PE.wait(k)
                for m in range(2):
                    a = (wh[:, j % 4, 128 * m:128 * m + 128], wl[:, j % 4, 128 * m:128 * m + 128])
                    f = mm3(bk[m].t[:, 0:124], a, (hi[:, :], lo[:, :]), j == 0, j == 15)
                    if m == 0:
                        PE.plain(f)
                k = PE.do(f)
                b.free = [k]
                if j % 4 == 3:
                    spent(i, k)
            for m in range(2):
                AC.wait(k)
                th = AC.do(lambda e, c=c, m=m, bk=bk: e.activation(hdn[:, c, m, :], bk[m].t[:, 0:124],
                                                                   ACT.Gelu_apprx_tanh))
                bk[m].free = [th]
        o = psr.next()
        t = o.take(PE)
        PE.wait(th, tw)
        for m in range(2):
            f = mm(t[:, 0:124], w2[:, 0, m, :, :].rearrange("p a d -> p (a d)"), hdn[:, 0, m, :], m == 0, m == 1)
            if m == 0:
                PE.plain(f)
        k = PE.do(f)
        V.wait(k)
        tkc = V.do(lambda e, t=t: e.tensor_copy(kc[:, :, :], t[:, 0:124].rearrange("p (g n) -> p g n", g=4)))
        o.free = [tkc]
        o = psr.next()
        t = o.take(PE)
        for g in range(4):
            for m in range(2):
                f = mm(t[0:31, 64 * g:64 * g + 64], hdn[:, 1, m, 31 * g:31 * g + 31], w2[:, 1, m, 0, :],
                       g == 0 and m == 0, m == 1)
                if not (g == 3 and m == 1):
                    PE.plain(f)
        k = PE.do(f)
        V.wait(k)
        tvc = V.do(lambda e, t=t: e.tensor_copy(vc[:, :, :], t[0:31, 0:256].rearrange("p (g n) -> p g n", g=4)))
        o.free = [tvc]
        fence()
        pe = Phase(r3, "ne")
        tmp.bufs = tmp.bufs + [Buf(pe.sb(f"t{i}", [128, S])) for i in range(6)]
        tmp.i = 0
        assert pe.at <= r4
        sc = 0.125
        scr, ptr = Ring(PS[0:3]), Ring(PS[3:6])
        steps = []
        for h in range(16):
            steps.append((h, -1))
            for i in (3, 2, 1, 0):
                steps.append((h, i))
        live, ob, held = {}, {}, []

        def a_(n):
            h, i = steps[n]
            g, c, p0 = h // 4, h // 2, 64 * (h % 2)
            w_ = sm.next()
            w = w_.take(V)
            PE.wait(kdt[("q", c)])
            if i < 0:
                o = scr.next()
                t = o.take(PE)
                PE.wait(tkc)
                for ti in range(4):
                    f = mm(t[:, 32 * ti:32 * ti + 31], q[p0:p0 + 64, c, 128 * ti:128 * ti + 128],
                           kc[p0:p0 + 64, g, :], ti == 0, False)
                    PE.plain(f)
                k = PE.do(mm(t[:, 0:128].rearrange("p (i n) -> p i n", i=4)[:, :, 0:31], Ib[:, :],
                             maskb[:, 3, :].rearrange("p (i n) -> p i n", i=4)[:, :, 0:31], False, True))
                tv_ = t[:, 0:128].rearrange("p (i n) -> p i n", i=4)[:, :, 0:31]
                p = tmp.next()
                pt = p.take(V)
                pv = pt[:, 0:128].rearrange("p (i n) -> p i n", i=4)[:, :, 0:31]
                V.wait(k)
                k = V.do(lambda e: e.tensor_reduce(w[:, 0:4], tv_, AX.X, ALU.max))
                V.wait(k)
                k = V.do(lambda e: e.tensor_tensor(pv, tv_, w[:, 0:4].unsqueeze(2).to_broadcast([128, 4, 31]),
                                                   ALU.subtract))
                o.free = [k]
                AC.wait(k)
                k = AC.do(lambda e: e.activation(pv, pv, ACT.Exp, scale=sc))
                live[n] = (w_, k, p, pv)
                return
            N = 128 * (i + 1)
            bks = []
            for kind in range(2):
                o = scr.next()
                t = o.take(PE)
                PE.wait(kdt[("k", kind, g)])
                PE.plain(mm(t[:, 0:N], qr[p0:p0 + 64, c, 128 * i:128 * i + 128], kd[kind][p0:p0 + 64, g, 0:N],
                            True, False))
                k = PE.do(mm(t[:, N - 128:N], Ib[:, :], maskb[:, 1, :], False, True))
                bks.append((o, t))
                V.wait(k)
                k = V.do(lambda e, kind=kind, t=t: e.reduce_max(w[:, kind:kind + 1], t[:, 0:N], AX.X))
            V.wait(k)
            k = V.do(lambda e: e.tensor_scalar(w[:, 2:4], w[:, 0:2], -sc, None, ALU.mult))
            AC.wait(k)
            ps_ = []
            for kind in range(2):
                o, t = bks[kind]
                p = tmp.next()
                pt = p.take(AC)
                k = AC.do(lambda e, kind=kind, t=t, pt=pt: e.activation(
                    pt[:, 0:N], t[:, 0:N], ACT.Exp, bias=w[:, 2 + kind:3 + kind], scale=sc,
                    accum_out=w[:, 4 + kind:5 + kind]))
                o.free = [k]
                ps_.append((p, pt))
            live[n] = (w_, k, ps_)

        def a2_(n):
            h, i = steps[n]
            w_, k = live[n][0:2]
            w = w_.t
            V.wait(k)
            if i < 0:
                p, pv = live[n][2:4]
                k = V.do(lambda e: e.tensor_reduce(w[:, 4:8], pv, AX.X, ALU.add))
                V.wait(k)
                k = V.do(lambda e: e.reciprocal(w[:, 8:12], w[:, 4:8]))
                V.wait(k)
                k = V.do(lambda e: e.tensor_tensor(w[:, 12:16], w[:, 8:12], gat[:, :, h], ALU.mult))
                V.wait(k)
                k = V.do(lambda e: e.tensor_tensor(pv, pv, w[:, 12:16].unsqueeze(2).to_broadcast([128, 4, 31]),
                                                   ALU.mult))
                w_.free = [k]
                live[n] = [(p, k)]
                return
            N = 128 * (i + 1)
            ps_ = live[n][2]
            out = []
            k = V.do(lambda e: e.reciprocal(w[:, 6:8], w[:, 4:6]))
            V.wait(k)
            k = V.do(lambda e: e.tensor_tensor(w[:, 8:10], w[:, 6:8], gat[:, i, 16 + h:16 + h + 17:16], ALU.mult))
            V.wait(k)
            for kind in range(2):
                p, pt = ps_[kind]
                k = V.do(lambda e, kind=kind, pt=pt: e.tensor_scalar(pt[:, 0:N], pt[:, 0:N], w[:, 8 + kind:9 + kind],
                                                                     None, ALU.mult))
                out.append((p, k))
            w_.free = [k]
            live[n] = out

        def b_(n):
            h, i = steps[n]
            g, c, p0 = h // 4, h // 2, 64 * (h % 2)
            if i < 0:
                (p, k), = live.pop(n)
                o = ptr.next()
                k = transposes(o, [(128 * ti, 31, p.t[:, 32 * ti:32 * ti + 31], con("I")) for ti in range(4)], [k])
                p.free = [k]
                ptc.take(AC)
                AC.wait(k, t_z)
                k = AC.do(lambda e: e.copy(ptc.t[:, 31:S], o.t[0:31, 31:S]))
                o.free = [k]
                if h % 2 == 0:
                    ob[0] = PS[6 + (h // 2) % 2]
                    ob[0].take(PE)

                def pv(o=ob[0], k=k):
                    PE.wait(k, tvc)
                    ptc.free = [PE.do(mm(o.t[p0:p0 + 64, :], vc[:, g, :], ptc.t[:, :], True, False))]
                held.append(pv)
                return
            for kind, (p, k) in enumerate(live.pop(n)):
                o = ptr.next()
                k = transposes(o, [(128 * j, 128, p.t[:, 128 * j:128 * j + 128], con("I")) for j in range(i + 1)], [k])
                p.free = [k]
                Q = (AC, V)[kind]
                if i == 3:
                    if kind == 0:
                        PTS.take(AC)
                        V.wait(PTS.was)
                Q.wait(k)
                dst = pts[:, kind, 0:i + 1, 128 * i:128 * i + 128]
                src = o.t[:, 0:128 * (i + 1)].rearrange("p (j t) -> p j t", t=128)
                k = Q.do((lambda e, dst=dst, src=src: e.copy(dst, src)) if kind == 0 else
                         (lambda e, dst=dst, src=src: e.tensor_copy(dst, src)))
                o.free = [k]
                live.setdefault("pt", []).append(k)
            if i == 0:
                def pv(o=ob[0], ks=live.pop("pt")):
                    PE.wait(tv, *ks)
                    for kind in range(2):
                        for j in range(4):
                            f = mm(o.t[p0:p0 + 64, 128 * j:512], vs[kind][:, j, 64 * g:64 * g + 64],
                                   pts[:, kind, j, 128 * j:512], False, kind == 1 and j == 3)
                            if not (kind == 1 and j == 3):
                                PE.plain(f)
                    k = PE.do(f)
                    PTS.free = [k]
                    PTS.was = k
                    if h % 2:
                        o.free = [split(OPx, c, o.t[:, :], k)]
                held.append(pv)

        PTS.was = None
        t_z = V.do(lambda e: e.memset(ptc.t[:, 0:31], 0.0))
        PE.wait(t_z)
        for n in range(len(steps)):
            was = held[:]
            held.clear()
            a_(n)
            for f in was:
                f()
            if n >= 3:
                b_(n - 3)
            if n >= 1:
                a2_(n - 1)
        a2_(len(steps) - 1)
        for n in (3, 2, 1):
            b_(len(steps) - n)
            while held:
                held.pop(0)()
        del tmp.bufs[4:]
        Ro = Runner()
        fence()
        for o in range(8):
            def leave(bank, tok, o=o):
                bank.free = [add_h(o, bank.t[:, :], tok)]
                after(o)
            Ro.push(lambda b, o=o: project(f"no{o}", OPx, b), leave)
        release(OPx)
        Ro.flush()

    def final(gain, n9):
        while n9.k < 8:
            n9.sum_step()
        n9.token()
        fence()
        ot = Phase(PH0, "fi").sb("ot", [128, 4, D])
        for k in range(8):
            AC.wait(htok[k], *hread[k])
            htok[k] = AC.do(lambda e, k=k: e.activation(H[:, k, :], H[:, k, :], ACT.Copy, scale=col(gain, k)))
        d_out = dsem("d_out")
        for i in range(4):
            done_ = []
            for half in range(2):
                o = psr.next()
                t = transposes(o, [(128 * (k % 4), 128, H[:, k, 128 * i:128 * i + 128], con("I"))
                                   for k in range(4 * half, 4 * half + 4)], [htok[4 * half + 3]])
                dst = ot[:, i, 512 * half:512 * half + 512]
                q = (AC, V)[half]
                q.wait(t, n9.rtok)
                if half == 0:
                    t = AC.do(lambda e, i=i, o=o, dst=dst: e.activation(dst, o.t[:, :], ACT.Copy,
                                                                        scale=n9.inv[:, i:i + 1]))
                else:
                    t = V.do(lambda e, i=i, o=o, dst=dst: e.tensor_scalar(dst, o.t[:, :], n9.inv[:, i:i + 1], None,
                                                                          ALU.mult))
                o.free = [t]
                done_.append(t)
            SP.wait(*done_)
            t_out = SP.dma(d_out, lambda e, i=i: e.dma_start(out_d[0, 128 * i:128 * i + 128, :], ot[:, i, :]))
        SP.wait(t_out)


    n_x = Norm(1e-6)
    n_f = Norm(1e-6)
    n_1 = Norm(1e-6)
    n_sb = Norm(1e-5)
    n_m0 = Norm(1e-5)
    n_ns = Norm(1e-5)
    n_m1 = Norm(1e-5)

    n_9 = Norm(1e-5)

    def squares_all(norm):
        for k in range(8):
            squares(norm)(k)

    def nothing(k):
        pass

    def squares(norm):
        def f(k):
            hread[k] = [norm.square(H[:, k, :], htok[k])]
            while norm.k < len(norm.sq) - 1:
                norm.sum_step()
        return f

    def between():
        while n_1.k < 8:
            n_1.sum_step()
        n_1.finish(tmp.next())
        g = normed(n_sb, "ng", 0, X)
        for k in range(8):
            V.wait(n_1.tok, htok[k], *hread[k])
            htok[k] = V.do(lambda e, k=k: e.scalar_tensor_tensor(H[:, k, :], H[:, k, :], col("first", k),
                                                                 rs.t[:, :], ALU.mult, ALU.mult))
            rs.free = [htok[k]]
            g(k)

    f_kv, f_q = None, None

    def both(k):
        hread[k] = [n_ns.square(H[:, k, :], htok[k])]
        hread[k].append(split(X, k, H[:, k, :], htok[k], col("kv_norm", k)))
        hread[k].append(split(XB, k, H[:, k, :], htok[k], col("ng", 16 + k)))
        while n_ns.k < len(n_ns.sq) - 1:
            n_ns.sum_step()

    def run_all():
        mixer(nothing if stop == "mixer" else normed(n_x, "xattn_norm"))
        if stop == "mixer":
            return
        xattn(n_x, nothing if stop == "xattn" else normed(n_f, "ffn_norm"))
        if stop == "xattn":
            return
        ffn("f", GU, X, n_f, PH0, nothing if stop == "ffn" else squares(n_1), True)
        if stop == "ffn":
            return
        between()
        stick(X, n_sb, X, nothing if stop == "stick" else normed(n_m0, "ng", 8, XB))
        if stop == "stick":
            return
        ffn("m", [4] * 8, XB, n_m0, PH0 + 8 * S * 8, nothing if stop == "mlp0" else both, False)
        if stop == "mlp0":
            return
        nsa(X, XB, n_ns, X, nothing if stop == "nsa" else normed(n_m1, "ng", 24, XB))
        if stop == "nsa":
            return
        ffn("n", [4] * 8, XB, n_m1, PH0 + 8 * S * 8, squares(n_9), False)

    run_all()
    if stop:
        squares_all(n_9)
    final("final", n_9)
    assert stop or at[0] == len(U)

    with nc.Block() as block:
        @block.sync
        def _(e):
            for f in SP.ops:
                f(e)

        @block.tensor
        def _(e):
            for f in PE.ops:
                f(e)

        @block.vector
        def _(e):
            for f in V.ops:
                f(e)

        @block.scalar
        def _(e):
            for f in AC.ops:
                f(e)

        @block.gpsimd
        def _(e):
            for f in PL.ops:
                f(e)


_INS = ["x", "mem", "w_in", "pool_w", "w_out_mix", "w_q", "w_kv", "w_o", "w_gate_up", "w_down",
        "sb_w_qkv_2", "sb_w_o_2", "nsa_w_kv_2", "cmp_w1_2", "cmp_w2_2", "nsa_w_q_2", "nsa_w_o_2",
        "mlp_w1_2", "mlp_w2_2"]


def columns(a):
    c = np.zeros((128, NCOLS), np.float32)

    def put(name, v):
        at, w = COLS[name]
        c[:, at:at + w] = v

    def feat(v):
        return np.asarray(v).reshape(-1, 128).T

    for name, v in (("mix_norm", a["mix_norm"]), ("conv_b", a["conv_b"]), ("ssd_norm", a["ssd_norm"]),
                    ("pool_scale", a["pool_scale"]), ("xattn_norm", a["xattn_norm"]),
                    ("mem_norm", a["mem_norm"]), ("ffn_norm", a["ffn_norm"]), ("kv_norm", a["kv_norm_2"]),
                    ("first", a["final_norm"]), ("final", a["final_norm_2"]), ("ng", a["norm_gain_2"]),
                    ("conv_w", a["conv_w"])):
        put(name, feat(v))
    put("d_skip", feat(np.repeat(np.asarray(a["d_skip"]).reshape(-1), 64)))
    pos = np.asarray(a["cmp_pos_2"]).reshape(2, 16, 2, 64)
    put("cmp_pos", pos.transpose(2, 3, 0, 1).reshape(128, 32))
    put("dt_bias", np.tile(np.asarray(a["dt_bias"]).reshape(1, 16), (128, 1)))
    put("a_log", np.tile(np.asarray(a["a_log"]).reshape(1, 16), (128, 1)))
    put("gate_b", np.tile(np.asarray(a["nsa_gate_b_2"]).reshape(1, 48), (128, 1)))
    return c


def kernel(**inputs):
    import concourse.bacc as bacc
    from concourse.bass_utils import run_bass_kernel_spmd

    nc = bacc.Bacc("TRN2", target_bir_lowering=False, num_devices=1)
    arrays = {f"in_{n}": np.ascontiguousarray(inputs[n]) for n in _INS}
    arrays["in_cols"] = columns(inputs)
    arrays["in_const"] = constants()
    aps = {n: nc.dram_tensor(n, a.shape, F, kind="ExternalInput").ap() for n, a in arrays.items()}
    out = nc.dram_tensor("out_0", (1, S, D), F, kind="ExternalOutput").ap()
    program(nc, {n: aps[f"in_{n}"] for n in _INS}, aps["in_cols"], aps["in_const"], out)
    r = run_bass_kernel_spmd(nc, [arrays], core_ids=[0])
    return r.results[0]["out_0"]
```

```python
import concourse.bass as bass
from concourse import mybir
import numpy as np

F = mybir.dt.float32
R = mybir.dt.float32r
BF = mybir.dt.bfloat16
ALU = mybir.AluOpType
ACT = mybir.ActivationFunctionType
AX = mybir.AxisListType

S, D, ML = 512, 1024, 256
NEG = -1.0e30

COLS = {}
_at = 0
for _n, _w in [("mix_norm", 8), ("conv_w", 48), ("conv_b", 12), ("ssd_norm", 8), ("pool_scale", 8),
               ("xattn_norm", 8), ("mem_norm", 8), ("ffn_norm", 8), ("kv_norm", 8), ("ng", 32),
               ("first", 8), ("final", 8), ("d_skip", 8), ("cmp_pos", 32), ("dt_bias", 16), ("a_log", 16),
               ("gate_b", 48)]:
    COLS[_n] = (_at, _w)
    _at += _w
NCOLS = _at

CONST = {}
_at = 0
for _n, _w in [("I", 128), ("TU", 128), ("TRI", 128), ("NONES", 128), ("ONES", 128), ("NEGT", 128),
               ("NEGC", 128), ("NEGS", 128), ("MS", 128), ("LAST", 128), ("CNT", 64), ("NEGM", 128),
               ("P", 128), ("D0", 128), ("D1", 128), ("PD0", 128), ("PD1", 128), ("RC", 512), ("RS", 512)]:
    CONST[_n] = (_at, _w)
    _at += _w
NCONST = _at


def constants():
    c = np.zeros((128, NCONST), np.float32)

    def put(name, a):
        at, w = CONST[name]
        c[:, at:at + w] = a

    i = np.arange(128)
    put("I", np.eye(128))
    put("TU", i[:, None] <= i[None, :])
    put("TRI", -1.0 * (i[:, None] >= i[None, :]))
    put("NONES", -1.0)
    put("ONES", 1.0)
    put("NEGT", NEG * (i[:, None] > i[None, :]))
    put("NEGC", NEG * (i[None, :] > i[:, None]))
    put("NEGS", NEG * (i[:, None] >= i[None, :]))
    put("MS", i[:, None] < i[None, :])
    put("LAST", (i[:, None] == 127) * np.ones((1, 128)))
    P = np.zeros((128, 128), np.float32)
    for base in (0, 64):
        for j in range(8):
            P[base + j + 8, base + j] = -1.0
            P[base + j, base + j + 8] = 1.0
    put("P", P)
    for g in range(2):
        Dg = np.zeros((128, 128), np.float32)
        for j in range(128):
            Dg[64 * g + j % 64, j] = 1.0
        put(f"D{g}", Dg)
        put(f"PD{g}", P @ Dg)
    for n, w in enumerate((2, 4, 8, 16)):
        at = CONST["CNT"][0] + 16 * n
        c[:, at:at + w] = np.float32(w) / np.arange(1, w + 1, dtype=np.float32)
    n = np.arange(32)
    for b in range(4):
        t = 128 * b + i
        at = CONST["NEGM"][0] + 32 * b
        c[:, at:at + 32] = NEG * ((16 * n + 31)[None, :] > t[:, None])
    inv = np.float32(500000.0) ** (-np.arange(8, dtype=np.float32) * np.float32(2.0) / np.float32(16))
    ang = np.arange(S, dtype=np.float32)[None, :] * inv[:, None].astype(np.float32)
    rc = np.ones((128, S), np.float32)
    rs = np.zeros((128, S), np.float32)
    for base in (0, 64):
        for o in (0, 8):
            rc[base + o:base + o + 8] = np.cos(ang)
            rs[base + o:base + o + 8] = np.sin(ang)
    put("RC", rc)
    put("RS", rs)
    return c


class Queue:

    def __init__(self, sem):
        self.sem, self.n, self.ops, self.seen = sem, 0, [], {}

    def wait(self, *tokens):
        for t in tokens:
            if t is None:
                continue
            if isinstance(t, list):
                self.wait(*t)
                continue
            sem, v = t
            if self.seen.get(sem.name, 0) < v:
                self.seen[sem.name] = v
                self.ops.append(lambda e, sem=sem, v=v: e.wait_ge(sem, v))

    def do(self, f):
        self.n += 1
        self.ops.append(lambda e: f(e).then_inc(self.sem, 1))
        return (self.sem, self.n)

    def plain(self, f):
        self.ops.append(f)

    def dma(self, sem, f):
        sem[1] += 16
        self.ops.append(lambda e, s=sem[0]: f(e).then_inc(s, 16))
        return (sem[0], sem[1])

    def now(self):
        return (self.sem, self.n) if self.n else None


class Buf:

    def __init__(self, t):
        self.t, self.last, self.live = t, [], False

    @property
    def free(self):
        return self.last

    @free.setter
    def free(self, tokens):
        self.last, self.live = tokens, False

    def take(self, *qs):
        assert not self.live
        for q in qs:
            q.wait(*self.last)
        self.last, self.live = [], True
        return self.t


class Ring:
    def __init__(self, bufs):
        self.bufs, self.i = bufs, 0

    def next(self):
        b = self.bufs[self.i % len(self.bufs)]
        self.i += 1
        return b


class Pair:

    def __init__(self, hi, lo, n):
        self.hi, self.lo, self.tok, self.free = hi, lo, [None] * n, [[] for _ in range(n)]


def program(nc, A, cols_d, const_d, out_d, stop=None):
    NR, NH = 5, 3
    base = [(nc.sbuf_base + 63) // 64 * 64]
    limit = nc.sbuf_usable_end

    def place(at, name, shape, dt=F):
        return nc.alloc_sbuf_tensor_at(name, shape, dt, offset=at)

    def size(shape, dt=F):
        n = 4 if dt != BF else 2
        for x in shape[1:]:
            n *= x
        return (n + 63) // 64 * 64

    def sb(name, shape, dt=F):
        t = place(base[0], name, shape, dt)
        base[0] += size(shape, dt)
        assert base[0] <= limit, (name, base[0], limit)
        return t

    class Phase:

        def __init__(self, at, tag):
            self.at, self.tag = at, tag

        def sb(self, name, shape, dt=F):
            t = place(self.at, f"{self.tag}_{name}", shape, dt)
            self.at += size(shape, dt)
            assert self.at <= limit, (name, self.at, limit)
            return t

    sems = {}

    def sem(name):
        sems[name] = nc.alloc_semaphore(name)
        return sems[name]

    PE, V, AC, PL, SP = (Queue(sem(f"done_{n}")) for n in ("pe", "dve", "act", "pool", "sp"))

    cols = sb("cols", [128, NCOLS])
    cst = sb("cst", [128, CONST["P"][0]])
    maskb = sb("maskb", [128, 4, 128], BF)
    Ib = sb("Ib", [128, 128], BF)
    small = sb("small", [128, 64])
    trir = sb("trir", [128, 2, 128], R)
    H = sb("H", [128, 8, S])
    RAW = [sb(f"raw{i}", [128, 1024]) for i in range(NR)]
    WH = [sb(f"wh{i}", [128, 1024], R) for i in range(NH)]
    WL = [sb(f"wl{i}", [128, 1024], R) for i in range(NH)]
    XH = sb("XH", [128, 8, S], R)
    XL = sb("XL", [128, 8, S], R)
    rs = Buf(sb("rs", [128, S]))
    sqr = Ring([Buf(sb(f"sq{i}", [128, S])) for i in range(2)])
    tmp = Ring([Buf(sb(f"tmp{i}", [128, S])) for i in range(4)])
    nrms = sb("nrms", [128, 80])
    sb_small = sb("sb_small", [128, 64])
    PH0 = base[0]
    X = Pair(XH, XL, 8)
    PS = [Buf(nc.alloc_psum_tensor(f"ps{i}", [128, 512], F)) for i in range(8)]
    psr = Ring(PS[0:7])
    NB = PS[7]

    def col(name, k, n=1, p=128):
        at, _ = COLS[name]
        return cols[0:p, at + k:at + k + n]

    def con(name, p0=0, p1=128, a=0, b=None):
        at, w = CONST[name]
        return cst[p0:p1, at + a:at + (w if b is None else b)]

    def dsem(name):
        return [sem(name), 0]

    U = []

    plain_units = set()

    def unit(name, ap, plain=False):
        if plain:
            plain_units.add(len(U))
        U.append((name, ap))

    def wcols(w, c0, n=128, r0=0, r1=None):
        v = w[r0:(r1 if r1 is not None else w.shape[0]), :].rearrange("(k p) n -> p k n", p=128)
        return v[:, :, c0:c0 + n]

    w_in, w_out = A["w_in"][0], A["w_out_mix"][0]
    unit("dt", wcols(w_in, 2560))
    for k in range(8):
        unit(f"v{k}", wcols(w_in, 2576 + 128 * k))
    def unit_pool(half):
        for g in (2 * half, 2 * half + 1):
            unit(f"pool{g}", wcols(A["pool_w"][0, g], 0, 256))

    def unit_out_pool(half):
        for o in range(4):
            unit(f"op{half}{o}", wcols(w_out, 256 * o, 256, 1024 + 512 * half, 1536 + 512 * half))

    unit_pool(0)
    for k in range(8, 12):
        unit(f"xbc{k}", wcols(w_in, 1024 + 128 * k))
    unit_out_pool(0)
    unit_pool(1)
    for k in range(8):
        unit(f"xbc{k}", wcols(w_in, 1024 + 128 * k))
        if k == 1:
            unit_out_pool(1)
    for k in range(8):
        unit(f"z{k}", wcols(w_in, 128 * k))
    for o in range(8):
        unit(f"os{o}", wcols(w_out, 128 * o, 128, 0, 1024))
    w_kv = A["w_kv"][0]
    for o in range(8):
        unit(f"mk{o}", wcols(w_kv, 128 * o))
    for b in range(2):
        for kk in range(4):
            unit(f"mv{b}{kk}", wcols(w_kv, 1024 + 512 * b, 512, 256 * kk, 256 * kk + 256))
    for o in range(8):
        unit(f"xq{o}", wcols(A["w_q"][0], 128 * o))
    for o in range(8):
        unit(f"xo{o}", wcols(A["w_o"][0], 128 * o))
    GU = [4, 4, 4, 4, 4, 2]
    wgu, wdn = A["w_gate_up"][0], A["w_down"][0]

    def ffn_order(groups):
        out = []
        for g in range(len(groups) + 1):
            if g < len(groups):
                out.append(("up", g))
            if g >= 1:
                out.append(("down", g - 1))
        return out

    def down_units(tag, w, g, c0, n):
        if n == 4:
            for o in range(4):
                unit(f"{tag}d{g}_{o}", wcols(w, 256 * o, 256, 128 * c0, 128 * (c0 + 4)))
        else:
            for o in range(2):
                unit(f"{tag}d{g}_{o}", wcols(w, 512 * o, 512, 128 * c0, 128 * (c0 + 2)))

    for kind, g in ffn_order(GU):
        c0 = sum(GU[:g])
        if kind == "up":
            for c in range(c0, c0 + GU[g]):
                unit(f"fg{c}", wcols(wgu, 128 * c))
                unit(f"fu{c}", wcols(wgu, 2816 + 128 * c))
        else:
            down_units("f", wdn, g, c0, GU[g])
    sbq = A["sb_w_qkv_2"][0]
    for o in range(16):
        unit(f"sq{o}", wcols(sbq, 128 * o))
    for b in range(2):
        for kk in range(4):
            unit(f"sv{b}{kk}", wcols(sbq, 2048 + 512 * b, 512, 256 * kk, 256 * kk + 256))
    for o in range(8):
        unit(f"so{o}", wcols(A["sb_w_o_2"][0], 128 * o))

    def mlp_units(tag, l):
        for kind, g in ffn_order([4] * 8):
            if kind == "up":
                for c in range(4 * g, 4 * g + 4):
                    unit(f"{tag}u{c}", wcols(A["mlp_w1_2"][l], 128 * c))
            else:
                down_units(tag, A["mlp_w2_2"][l], g, 4 * g, 4)

    mlp_units("m", 0)
    nq = A["nsa_w_q_2"][0]
    for o in range(8):
        unit(f"nq{o}", wcols(nq, 128 * o))
    unit("ng", wcols(nq, 1024, 48))
    nkv = A["nsa_w_kv_2"]
    for o in range(4):
        unit(f"nc{o}", wcols(nkv, 128 * o))
    for kind in range(2):
        for o in range(2):
            unit(f"nk{kind}{o}", wcols(nkv, 512 + 512 * kind + 128 * o))
    for kind in range(2):
        for kk in range(2):
            unit(f"nv{kind}{kk}", wcols(nkv, 768 + 512 * kind, 256, 512 * kk, 512 * kk + 512))
    for c in range(2):
        for j in range(4):
            unit(f"c1{c}{j}", wcols(A["cmp_w1_2"][c], 0, 256, 512 * j, 512 * j + 512), plain=True)
    for o in range(8):
        unit(f"no{o}", wcols(A["nsa_w_o_2"][0], 128 * o))
    mlp_units("n", 1)

    wsem = [dsem(f"w_in_{i}") for i in range(NR)]
    loaded, hi_done, lo_done, used = {}, {}, {}, {}
    at = [0, 0]

    def shaped(t, ap):
        n = ap.shape[1] * ap.shape[2]
        return t[:, 0:n].rearrange("p (k n) -> p k n", k=ap.shape[1])

    def issue(i):
        if i >= len(U):
            return
        if i >= NR:
            SP.wait(hi_done[i - NR], lo_done[i - NR])
        ap = U[i][1]
        loaded[i] = SP.dma(wsem[i % NR], lambda e: e.dma_start(shaped(RAW[i % NR], ap), ap))

    def prepare(i):
        if i >= len(U) or i in plain_units:
            return
        raw, wh, wl = (shaped(t, U[i][1]) for t in (RAW[i % NR], WH[i % NH], WL[i % NH]))
        for q in (AC, V):
            q.wait(loaded[i])
            if i >= NH:
                q.wait(used[i - NH])
        hi_done[i] = AC.do(lambda e: e.copy(wh, raw))
        V.wait(hi_done[i])
        lo_done[i] = V.do(lambda e: e.tensor_tensor(wl, raw, wh.bitcast(F), ALU.subtract))
        issue(i + NR)

    def weights(name):
        i = at[0]
        at[0] += 1
        assert U[i][0] == name, (U[i][0], name)
        while at[1] < min(i + 3, len(U)):
            prepare(at[1])
            at[1] += 1
        if i in plain_units:
            PE.wait(loaded[i])
            return i, shaped(RAW[i % NR], U[i][1])
        PE.wait(lo_done[i])
        return i, shaped(WH[i % NH], U[i][1]), shaped(WL[i % NH], U[i][1])

    def spent(i, tok):
        used[i] = tok
        if i in plain_units:
            hi_done[i] = lo_done[i] = tok
            issue(i + NR)

    def mm(out, a, b, start, stop):
        return lambda e: e.matmul(out, a, b, start=start, stop=stop, skip_group_check=True)

    def mm3(out, a, b, start=False, stop=False):
        PE.plain(mm(out, a[0], b[0], start, False))
        PE.plain(mm(out, a[0], b[1], False, False))
        return mm(out, a[1], b[0], False, stop)

    def project(name, x, bank, nk=8, c=0, k0=0, n=S, m=128):
        i, wh, wl = weights(name) if isinstance(name, str) else name
        out = bank.take(PE)[0:m, 0:n]
        for k in range(nk):
            PE.wait(x.tok[k0 + k])
            a = (wh[:, k, c:c + m], wl[:, k, c:c + m])
            f = mm3(out, a, (x.hi[:, k0 + k, 0:n], x.lo[:, k0 + k, 0:n]), k == 0, k == nk - 1)
            if k < nk - 1:
                PE.plain(f)
        tok = PE.do(f)
        spent(i, tok)
        return tok

    def split(x, k, src, tok, scale=None, n=S):
        hi, lo = x.hi[:, k, 0:n], x.lo[:, k, 0:n]
        AC.wait(tok, *x.free[k])
        V.wait(tok, *x.free[k])
        if scale is None:
            h = AC.do(lambda e: e.copy(hi, src))
            V.wait(h)
            x.tok[k] = V.do(lambda e: e.tensor_tensor(lo, src, hi.bitcast(F), ALU.subtract))
        else:
            h = AC.do(lambda e: e.activation(hi, src, ACT.Copy, scale=scale))
            V.wait(h)
            x.tok[k] = V.do(lambda e: e.scalar_tensor_tensor(lo, src, scale, hi.bitcast(F), ALU.mult,
                                                             ALU.subtract))
        x.free[k] = []
        return x.tok[k]

    ph = Phase(PH0, "p0")
    xt = ph.sb("xt", [128, 4, D])
    d_par = dsem("d_par")
    xv = A["x"][0].rearrange("(i p) d -> p i d", p=128)
    xtoks = []
    for n in range(4):
        q = (AC, SP)[n % 2]
        xtoks.append(q.dma(dsem(f"d_x{n}"), lambda e, n=n: e.dma_start(xt[:, n, :], xv[:, n, :])))
        if n == 0:
            t_id = AC.dma(dsem("d_id"), lambda e: e.dma_start(cst[:, 0:128], const_d[:, 0:128]))
    AC.dma(d_par, lambda e: e.dma_start(cst[:, 128:], const_d[:, 128:CONST["P"][0]]))
    t_par = AC.dma(d_par, lambda e: e.dma_start(cols[:, :], cols_d))
    for i in range(NR):
        issue(i)
    htok = [None] * 8
    hread = [[] for _ in range(8)]

    for k in range(8):
        b = psr.next()
        t = b.take(PE)
        PE.wait(t_id, *xtoks)
        for i in range(4):
            f = lambda e, i=i, k=k, t=t: e.transpose(t[:, 128 * i:128 * i + 128],
                                                     xt[:, i, 128 * k:128 * k + 128], con("I"))
            if i < 3:
                PE.plain(f)
        tk = PE.do(f)
        V.wait(tk)
        htok[k] = V.do(lambda e, k=k, t=t: e.tensor_copy(H[:, k, :], t[:, :]))
        b.free = [htok[k]]

    V.wait(t_par)
    V.plain(lambda e: e.memset(small[:, 0:1], 1e-6))
    V.plain(lambda e: e.memset(small[:, 1:2], 1e-5))
    V.plain(lambda e: e.memset(small[:, 2:3], 1.0))
    V.plain(lambda e: e.tensor_copy(Ib[:, :], con("I")))
    for n, name in enumerate(("NEGT", "NEGC", "NEGS", "NEGM")):
        V.plain(lambda e, n=n, name=name: e.tensor_copy(maskb[:, n, :], con(name)))
    V.plain(lambda e: e.tensor_copy(trir[:, 0, :], con("TRI")))
    t_const = V.do(lambda e: e.tensor_copy(trir[:, 1, :], con("NONES")))
    g12 = small[:, 8:16]
    gsq = small[:, 16:32].rearrange("p (k c) -> p k c", c=2)
    V.plain(lambda e: e.memset(gsq[:, :, 0], 1.0))
    V.plain(lambda e: e.tensor_tensor(gsq[:, :, 1], col("first", 0, 8), col("first", 0, 8), ALU.mult))
    t_const = V.do(lambda e: e.tensor_tensor(g12, col("first", 0, 8), col("ng", 0, 8), ALU.mult))
    for q in (PE, AC, PL):
        q.wait(t_const)
        q.wait(t_par)
    V.wait(t_const)
    EPS = {1e-6: small[:, 0:1], 1e-5: small[:, 1:2]}
    ONE1 = small[:, 2:3]

    norms = [0]

    class Norm:

        def __init__(self, eps, nk=8, want=True):
            self.eps, self.nk, self.k = eps, nk, 0
            self.at = norms[0]
            norms[0] += 8
            self.std = nrms[:, self.at:self.at + 4]
            self.inv = nrms[:, self.at + 4:self.at + 8]
            self.bank = None
            self.sq = []

        def square(self, src, tok):
            b = sqr.next()
            t = b.take(PL)
            PL.wait(tok)
            s = PL.do(lambda e: e.tensor_tensor(t[:, :], src, src, ALU.mult))
            self.sq.append((b, s))
            return s

        def sum_step(self):
            if self.bank is None:
                self.bank = NB
                self.bank.take(PE)
            b, s = self.sq[self.k]
            PE.wait(s)
            for i in range(4):
                f = mm(self.bank.t[:, i:i + 1], b.t[:, 128 * i:128 * i + 128], con("ONES", b=1),
                       self.k == 0 and i == 0, self.k == self.nk - 1)
                if i < 3:
                    PE.plain(f)
            self.last = PE.do(f)
            b.free = [self.last]
            self.k += 1

        def token(self):
            AC.wait(self.last)
            a = AC.do(lambda e: e.activation(self.std, self.bank.t[:, 0:4], ACT.Sqrt, bias=EPS[self.eps],
                                             scale=1.0 / 1024))
            NB.free = [a]
            V.wait(a)
            self.rtok = V.do(lambda e: e.reciprocal(self.inv, self.std))

        def finish(self, diag):
            self.token()
            self.tok = spread(self.inv, self.rtok, diag)

    class TwoNorms(Norm):

        def __init__(self, first):
            super().__init__(1e-5)
            self.first = first

        def square(self, src, tok):
            return self.first.square(src, tok)

        def sum_step(self):
            n = self.first
            if self.bank is None:
                self.bank = NB
                self.bank.take(PE)
            b, s = n.sq[self.k]
            PE.wait(s)
            for i in range(4):
                f = mm(self.bank.t[:, 2 * i:2 * i + 2], b.t[:, 128 * i:128 * i + 128], gsq[:, self.k, :],
                       self.k == 0 and i == 0, self.k == 7)
                if i < 3:
                    PE.plain(f)
            self.last = PE.do(f)
            b.free = [self.last]
            self.k += 1

        def token(self):
            n = self.first
            s = self.bank.t[:, 0:8].rearrange("p (i c) -> p c i", c=2)
            AC.wait(self.last)
            a = AC.do(lambda e: e.activation(n.std, s[:, 0, :], ACT.Sqrt, bias=EPS[1e-6], scale=1.0 / 1024))
            V.wait(a)
            n.rtok = V.do(lambda e: e.reciprocal(n.inv, n.std))
            V.wait(n.rtok)
            k = V.do(lambda e: e.tensor_tensor(n.std, s[:, 1, :], n.inv, ALU.mult))
            NB.free = [k]
            V.wait(k)
            k = V.do(lambda e: e.tensor_tensor(n.std, n.std, n.inv, ALU.mult))
            AC.wait(k)
            k = AC.do(lambda e: e.activation(self.std, n.std, ACT.Sqrt, bias=EPS[1e-5], scale=1.0 / 1024))
            V.wait(k)
            V.wait(V.do(lambda e: e.reciprocal(self.inv, self.std)))
            self.rtok = V.do(lambda e: e.tensor_tensor(self.inv, self.inv, n.inv, ALU.mult))

    def spread(inv, tok, diag):
        t = NB.take(PE)
        diag.take(V)
        V.wait(tok)
        for i in range(4):
            g = V.do(lambda e, i=i: e.tensor_scalar(diag.t[:, 128 * i:128 * i + 128], con("I"),
                                                    inv[:, i:i + 1], None, ALU.mult))
        PE.wait(g)
        for i in range(4):
            f = mm(t[:, 128 * i:128 * i + 128], con("ONES"), diag.t[:, 128 * i:128 * i + 128], True, True)
            if i < 3:
                PE.plain(f)
        m = PE.do(f)
        diag.free = [m]
        AC.wait(m, *rs.free)
        k = AC.do(lambda e: e.copy(rs.t[:, :], t[:, :]))
        NB.free = [k]
        return k

    def normed(norm, gain, goff=0, x=X):
        def f(k):
            hread[k] = [norm.square(H[:, k, :], htok[k])]
            hread[k].append(split(x, k, H[:, k, :], htok[k], col(gain, goff + k)))
            while norm.k < len(norm.sq) - 1:
                norm.sum_step()
        return f

    class Runner:

        def __init__(self, norm=None):
            self.norm, self.n, self.pend, self.late = norm, 0, [], []

        def push(self, f, g):
            b = psr.next()
            self.pend.append((g, b, f(b)))
            self.n += 1
            if self.norm is not None and self.n == 1:
                while self.norm.k < self.norm.nk:
                    self.norm.sum_step()
            if self.norm is not None and self.n == 2:
                self.norm.finish(tmp.next())
                self.norm = None
            if self.norm is None:
                self.drain(1)
            self.later(2)

        def drain(self, keep=0):
            while len(self.pend) > keep:
                g, b, t = self.pend.pop(0)
                r = g(b, t)
                if r is not None:
                    self.late.append((self.n, r))

        def later(self, lag):
            while self.late and self.late[0][0] + lag <= self.n:
                more = self.late.pop(0)[1]()
                if more is not None:
                    self.late.append((self.n, more))

        def flush(self):
            self.drain()
            self.later(-1000)

    def add_h(o, src, tok, *more):
        V.wait(tok, htok[o], *hread[o], *more)
        htok[o] = V.do(lambda e: e.tensor_tensor(H[:, o, :], H[:, o, :], src, ALU.add))
        hread[o] = []
        return htok[o]

    def add_scaled(o, bank, tok, norm):
        b = tmp.next()
        t = b.take(V)
        k = scaled(bank, tok, t[:, :], norm)
        b.free = [add_h(o, t[:, :], k)]

    def scaled(bank, tok, dst, norm, p=128):
        V.wait(tok, norm.tok)
        t = V.do(lambda e: e.tensor_tensor(dst, bank.t[0:p, :], rs.t[0:p, :], ALU.mult))
        bank.free = [t]
        rs.free = [t]
        return t

    def release(x):
        x.free = [[PE.now()] for _ in x.free]

    def fence():
        t = [q.now() for q in (PE, V, AC, PL)]
        for q in (V, AC, PL, SP):
            q.wait(*t)

    def transposes(dst, blocks, toks):
        t = dst.take(PE)
        PE.wait(*toks)
        for n, (o, p, src, ident) in enumerate(blocks):
            f = lambda e, o=o, p=p, src=src, ident=ident: e.transpose(t[0:p, o:o + src.shape[0]], src, ident)
            if n < len(blocks) - 1:
                PE.plain(f)
        return PE.do(f)

    sm = Ring([Buf(sb_small[:, 16 * i:16 * i + 16]) for i in range(4)])
    XB = Pair(*(Phase(PH0 + 4 * 8 * S * i, f"xb{i}").sb("x", [128, 8, S], R) for i in range(2)), 8)

    def mixer(after):
        n1 = Norm(1e-6)
        f = normed(n1, "mix_norm")
        for k in range(8):
            f(k)
        ph = Phase(PH0, "mx")
        r1 = ph.at
        dp = Pair(ph.sb("dh", [128, 8, S], R), ph.sb("dl", [128, 8, S], R), 8)
        ph1 = Phase(r1, "my")
        xsf = ph1.sb("xsf", [128, 8, S])
        r1b = ph1.at
        xc = ph1.sb("xc", [128, 4, D])
        bc = ph.sb("bc", [128, 4, S])
        btok = ph.sb("btok", [128, 4, 2, 128])
        cb = ph.sb("cb", [128, 2, S])
        r2 = ph.at
        yp = Pair(ph.sb("yh", [128, 4, S], R), ph.sb("yl", [128, 4, S], R), 4)
        prev = Phase(r2, "mz").sb("prev", [128, 3, D])
        z = ph.sb("z", [128, 8, S])
        pads = Ring([Buf(ph.sb(f"pad{i}", [128, 528])) for i in range(2)])
        dtt = ph.sb("dtt", [128, 10, 64])
        t_pad = None
        early = Phase(PH0 + 4 * 8 * S * 4, "mv")
        pads.bufs += [Buf(early.sb(f"p{i}", [128, 528])) for i in range(3)]
        sums = Ring([Buf(early.sb(f"s{i}", [128, 528])) for i in range(4)])
        for b in pads.bufs:
            t_pad = V.do(lambda e, b=b: e.memset(b.t[:, 0:16], 0.0))
        V.wait(t_pad)
        PL.wait(t_pad)
        ss = [Buf(ph.sb(f"ps{i}", [128, 528])) for i in range(2)]
        R1 = Runner(n1)

        def v_leave(k):
            def g(bank, tok):
                w = 2 << (k // 2)
                u = pads.next()
                t = u.take(V)
                a = scaled(bank, tok, t[:, 16:528], n1)
                src, cur, step = t, a, 1
                for n in range(k // 2 + 1):
                    d = ss[n % 2] if n < k // 2 else sums.next()
                    dt_ = d.take(PL)
                    PL.wait(cur)
                    lo = 2 * step - 1
                    cur = PL.do(lambda e, s_=src, d_=dt_, lo=lo, step=step: e.tensor_tensor(
                        d_[:, lo:528], s_[:, lo:528], s_[:, lo - step:528 - step], ALU.add))
                    src, step, last = dt_, 2 * step, d
                    if n:
                        ss[(n - 1) % 2].free = [cur]

                def late():
                    V.wait(cur)
                    at = CONST["CNT"][0] + 16 * (k // 2)
                    c = V.do(lambda e: e.tensor_tensor(src[:, 16:16 + w], src[:, 16:16 + w],
                                                       cst[:, at:at + w], ALU.mult))
                    V.wait(c)
                    b = tmp.next()
                    o = b.take(V)
                    c = V.do(lambda e: e.scalar_tensor_tensor(o[:, :], src[:, 16:528], 1.0 / w, t[:, 16:528],
                                                              ALU.mult, ALU.subtract))
                    last.free = [c]
                    u.free = [c]
                    b.free = [split(dp, k, o[:, :], c)]
                return late
            return g


        def tcol(i, p=128):
            return dtt[0:p, i, :]

        st = {}

        def dt_leave(bank, tok):
            b = tmp.next()
            t = b.take(V)
            a = scaled(bank, tok, t[0:16, :], n1, p=16)

            def late():
                o = psr.next()
                k = transposes(o, [(16 * i, 128, t[0:16, 128 * i:128 * i + 128], con("I", 0, 16, 0, 16))
                                   for i in range(4)], [a])
                b.free = [k]
                V.wait(k)
                v = lambda i: dtt[:, i, :].rearrange("p (c h) -> p c h", c=4)
                bias = col("dt_bias", 0, 16).unsqueeze(1).to_broadcast([128, 4, 16])
                k = V.do(lambda e: e.tensor_tensor(v(4), o.t[:, 0:64].rearrange("p (c h) -> p c h", c=4),
                                                   bias, ALU.add))
                o.free = [k]
                V.wait(k)
                AC.wait(k)
                AC.wait(AC.do(lambda e: e.activation(tcol(5), tcol(4), ACT.Abs)))
                k = AC.do(lambda e: e.activation(tcol(5), tcol(5), ACT.Exp, scale=-1.0))
                ka = AC.do(lambda e: e.activation(tcol(8)[:, 0:16], col("a_log", 0, 16), ACT.Exp))
                V.wait(k)

                def step(f):
                    V.wait(V.do(f))
                step(lambda e: e.tensor_scalar(tcol(6), tcol(5), 2.0, None, ALU.add))
                step(lambda e: e.reciprocal(tcol(6), tcol(6)))
                step(lambda e: e.tensor_tensor(tcol(5), tcol(5), tcol(6), ALU.mult))
                step(lambda e: e.tensor_tensor(tcol(6), tcol(5), tcol(5), ALU.mult))
                step(lambda e: e.tensor_scalar(tcol(7), tcol(6), 2.0 / 15, 2.0 / 13, ALU.mult, ALU.add))
                for n in (11, 9, 7, 5, 3, 1):
                    step(lambda e: e.tensor_tensor(tcol(7), tcol(7), tcol(6), ALU.mult))
                    step(lambda e, n=n: e.tensor_scalar(tcol(7), tcol(7), 2.0 / n, None, ALU.add))
                step(lambda e: e.tensor_tensor(tcol(7), tcol(7), tcol(5), ALU.mult))
                step(lambda e: e.scalar_tensor_tensor(tcol(0), tcol(4), 0.0, tcol(7), ALU.max, ALU.add))
                V.wait(ka)
                av = dtt[:, 8, 0:16].unsqueeze(1).to_broadcast([128, 4, 16])
                k = V.do(lambda e: e.scalar_tensor_tensor(v(1), v(0), -1.0, av, ALU.mult, ALU.mult))
                st["dt"] = k
                return lambda: (lambda: dt_sums(k))

            def dt_sums(k):
                o2 = psr.next()
                t2 = o2.take(PE)
                PE.wait(k)
                k = PE.do(mm(t2[:, 0:64], con("TU"), tcol(1), True, True))
                V.wait(k)
                AC.wait(k)
                k = V.do(lambda e: e.tensor_copy(tcol(2), t2[:, 0:64]))
                V.wait(k)
                st["neg"] = V.do(lambda e: e.tensor_scalar(tcol(3), tcol(2), -1.0, None, ALU.mult))
                PE.wait(k)
                k = PE.do(mm(t2[:, 64:128], con("LAST"), tcol(2), True, True))
                AC.wait(k)
                ed = AC.do(lambda e: e.activation(tcol(9), t2[:, 64:128], ACT.Exp))
                V.wait(k, ed)
                k = V.do(lambda e: e.tensor_tensor(tcol(6), t2[:, 64:128], tcol(2), ALU.subtract))
                AC.wait(k)
                k2 = AC.do(lambda e: e.activation(tcol(6), tcol(6), ACT.Exp))
                o2.free = [ed, k]
                st["dt"], st["decay"], st["ed"] = k, k2, ed
                return None
            return late

        R1.push(lambda b: project("dt", X, b), dt_leave)
        for k in range(8):
            R1.push(lambda b, k=k: project(f"v{k}", X, b), v_leave(k))

        def conv_leave(k, dst, nxt=None):
            def g(bank, tok):
                u = pads.next()
                t = u.take(V)
                a = scaled(bank, tok, t[:, 16:528], n1)
                b = tmp.next()
                o = b.take(AC)
                AC.wait(a, t_pad)
                w = lambda j: col("conv_w", 12 * j + k)
                c = AC.do(lambda e: e.activation(o[:, :], t[:, 13:525], ACT.Copy, scale=w(0)))
                for j in range(1, 4):
                    V.wait(c)
                    c = V.do(lambda e, j=j: e.scalar_tensor_tensor(
                        o[:, :], t[:, 13 + j:525 + j], w(j), o[:, :], ALU.mult, ALU.add))
                u.free = [c]
                AC.wait(c)
                s_ = AC.do(lambda e: e.activation(dst, o[:, :], ACT.Silu, bias=col("conv_b", k)))
                b.free = [s_]
                if nxt is None:
                    return None
                return lambda: nxt(s_)
            return g

        btk = {}

        def b_next(g):
            def f(s_):
                o = psr.next()
                k = transposes(o, [(128 * c, 128, bc[:, g, 128 * c:128 * c + 128], con("I"))
                                   for c in range(4)], [s_])
                V.wait(k)
                btk[g] = V.do(lambda e: e.tensor_copy(
                    btok[:, :, g, :], o.t[:, :].rearrange("p (c n) -> p c n", c=4)))
                o.free = [btk[g]]
            return f

        def c_next(g):
            def f(s_):
                btk[("c", g)] = s_
                o = psr.next()
                t = o.take(PE)
                PE.wait(s_)
                for c in range(4):
                    m = mm(t[:, 128 * c:128 * c + 128], bc[:, g, 128 * c:128 * c + 128],
                           bc[:, 2 + g, 128 * c:128 * c + 128], True, True)
                    if c < 3:
                        PE.plain(m)
                k = PE.do(m)
                AC.wait(k)
                btk[("cb", g)] = AC.do(lambda e: e.copy(cb[:, g, :], t[:, :]))
                o.free = [btk[("cb", g)]]
            return f


        def pool_jobs(g, base):
            cell = {}
            for m in range(2):
                def f(b, m=m):
                    if m == 0:
                        cell["u"] = weights(f"pool{g}")
                    return project(cell["u"], dp, b, nk=2, c=128 * m, k0=2 * g)

                def leave(bank, tok, m=m):
                    k = 2 * g + m
                    bank.free = [split(yp, k - base, bank.t[:, :], tok, col("pool_scale", k))]
                R1.push(f, leave)

        def out_pool(half):
            for o in range(4):
                cell = {}
                for m in range(2):
                    def f(b, o=o, m=m, cell=cell):
                        if m == 0:
                            cell["u"] = weights(f"op{half}{o}")
                        return project(cell["u"], yp, b, nk=4, c=128 * m)

                    def leave(bank, tok, o=o, m=m):
                        bank.free = [add_h(2 * o + m, bank.t[:, :], tok)]
                    R1.push(f, leave)
            release(yp)

        pool_jobs(0, 0)
        pool_jobs(1, 0)
        nx = [b_next(0), b_next(1), c_next(0), c_next(1)]
        for k in range(8, 12):
            R1.push(lambda b, k=k: project(f"xbc{k}", X, b), conv_leave(k, bc[:, k - 8, :], nx[k - 8]))
        out_pool(0)
        del pads.bufs[2:]
        pads.i = 0
        t_early = [V.now(), PL.now(), AC.now()]
        pool_jobs(2, 4)
        pool_jobs(3, 4)
        release(dp)
        t_dp = PE.now()
        AC.wait(t_dp)
        V.wait(t_dp)
        xtok, xctok = {}, {}

        def xs_next(k):
            def f(s_):
                xtok[k] = s_
                o = psr.next()
                q = transposes(o, [(128 * c, 128, xsf[:, k, 128 * c:128 * c + 128], con("I"))
                                   for c in range(4)], [s_])
                V.wait(q, st["dt"])
                src = o.t[:, :].rearrange("p (c j d) -> p c j d", c=4, j=2)
                dst = xc[:, :, 128 * k:128 * k + 128].rearrange("p c (j d) -> p c j d", j=2)
                dd = dtt[:, 0, :].rearrange("p (c h) -> p c h", c=4)[:, :, 2 * k:2 * k + 2]
                xctok[k] = V.do(lambda e: e.tensor_tensor(
                    dst, src, dd.unsqueeze(3).to_broadcast([128, 4, 2, 64]), ALU.mult))
                o.free = [xctok[k]]
            return f

        for k in range(8):
            R1.push(lambda b, k=k: project(f"xbc{k}", X, b), conv_leave(k, xsf[:, k, :], xs_next(k)))
            if k == 1:
                out_pool(1)
        t_yp = PE.now()

        ztok = {}

        def z_leave(k):
            def g(bank, tok):
                b = sqr.next()
                t = b.take(V)
                a = scaled(bank, tok, t[:, :], n1)
                AC.wait(a, *t_early)
                ztok[k] = AC.do(lambda e: e.activation(z[:, k, :], t[:, :], ACT.Silu))
                b.free = [ztok[k]]
            return g

        def z_job(k):
            R1.push(lambda b, k=k: project(f"z{k}", X, b), z_leave(k))
            if k == 7:
                release(X)

        z_job(0)
        z_job(1)
        z_job(2)
        R1.flush()
        V.wait(t_yp)
        ptok = {}
        dec = dtt[:, 6, :].rearrange("p (c h) -> p c h", c=4)
        edc = dtt[:, 9, :].rearrange("p (c h) -> p c h", c=4)
        PL.wait(st["decay"], *[xctok[k] for k in range(8)])
        def state_in(c, g):
            b = tmp.next()
            t = b.take(PL)
            return b, PL.do(lambda e: e.tensor_tensor(
                t[:, :].rearrange("p (h d) -> p h d", h=8),
                xc[:, c, 512 * g:512 * g + 512].rearrange("p (h d) -> p h d", h=8),
                dec[:, c, 8 * g:8 * g + 8].unsqueeze(2).to_broadcast([128, 8, 64]), ALU.mult))

        def state(c, g, b, xd):
            o = psr.next()
            bt = o.take(PE)
            PE.wait(xd, btk[g])
            k = PE.do(mm(bt[:, :], btok[:, c, g, :], b.t[:, :], True, True))
            b.free = [k]
            V.wait(k, st["ed"])
            dst = prev[:, c, 512 * g:512 * g + 512]
            if c == 0:
                ptok[(c, g)] = V.do(lambda e: e.tensor_copy(dst, bt[:, :]))
            else:
                V.wait(ptok[(c - 1, g)])
                k = V.do(lambda e: e.tensor_tensor(
                    dst.rearrange("p (h d) -> p h d", h=8),
                    prev[:, c - 1, 512 * g:512 * g + 512].rearrange("p (h d) -> p h d", h=8),
                    edc[:, c, 8 * g:8 * g + 8].unsqueeze(2).to_broadcast([128, 8, 64]), ALU.mult))
                V.wait(k)
                ptok[(c, g)] = V.do(lambda e: e.tensor_tensor(dst, dst, bt[:, :], ALU.add))
            o.free = [ptok[(c, g)]]

        order = [(c, g) for c in range(3) for g in range(2)]
        ins = [state_in(*cg) for cg in order[0:3]]
        z_job(3)
        for n, cg in enumerate(order):
            state(*cg, *ins[n])
            if n + 3 < 6:
                ins.append(state_in(*order[n + 3]))
            if n == 2:
                z_job(4)

        n2 = Norm(1e-6)
        YP = X
        adt = dtt[:, 1, :].rearrange("p (c h) -> p c h", c=4)
        nacs = dtt[:, 3, :].rearrange("p (c h) -> p c h", c=4)
        heads = {}

        def head_a(h):
            o = psr.next()
            t = o.take(PE)
            PE.wait(st["dt"])
            for c in range(4):
                m = mm(t[:, 128 * c:128 * c + 128], adt[:, c, h:h + 1].to_broadcast([128, 128]),
                       con("TU"), c == 0, False)
                if c < 3:
                    PE.plain(m)
            k = PE.do(m)
            eb = tmp.next()
            et = eb.take(AC)
            AC.wait(k, st["neg"])
            heads[h] = (o, eb, AC.do(lambda e: e.activation(et[:, :], t[:, :], ACT.Exp)))

        def head_m(h):
            g = h // 8
            o, eb, a = heads[h]
            t, et = o.t, eb.t
            PE.wait(a)
            for c in range(4):
                m = mm(t[:, 128 * c:128 * c + 128], Ib[:, :], maskb[:, 0, :], False, c == 3)
                if c < 3:
                    PE.plain(m)
            k = PE.do(m)
            sg = tmp.next()
            sgt = sg.take(AC)
            AC.wait(k)
            for c in range(4):
                s_ = AC.do(lambda e, c=c: e.activation(sgt[:, 128 * c:128 * c + 128],
                                                       t[:, 128 * c:128 * c + 128], ACT.Exp,
                                                       bias=nacs[:, c, h:h + 1]))
            o.free = [s_]
            PL.wait(a, btk[("c", g)])
            ce = PL.do(lambda e: e.tensor_tensor(et[:, :], bc[:, 2 + g, :], et[:, :], ALU.mult))
            V.wait(s_, btk[("cb", g)])
            m_ = V.do(lambda e: e.tensor_tensor(sgt[:, :], sgt[:, :], cb[:, g, :], ALU.mult))
            heads[h] = (eb, sg, ce, m_)

        ybank = {}

        def head_b(h):
            eb, sg, ce, m_ = heads.pop(h)
            g, p0 = h // 8, 64 * (h % 2)
            if h % 2 == 0:
                ybank[h // 2] = PS[5 + (h // 2) % 2]
                ybank[h // 2].take(PE)
            o = ybank[h // 2]
            PE.wait(ce, m_, xctok[h // 2], ptok[(2, g)])
            for c in range(4):
                out = o.t[p0:p0 + 64, 128 * c:128 * c + 128]
                PE.plain(mm(out, xc[:, c, 64 * h:64 * h + 64], sg.t[:, 128 * c:128 * c + 128],
                            c == 0, c == 0))
                if c:
                    m = mm(out, prev[:, c - 1, 64 * h:64 * h + 64], eb.t[:, 128 * c:128 * c + 128],
                           False, True)
                    if c < 3:
                        PE.plain(m)
            k = PE.do(m)
            eb.free = [k]
            sg.free = [k]
            if h % 2:
                j = h // 2
                V.wait(k, xtok[j])
                k = V.do(lambda e: e.scalar_tensor_tensor(xsf[:, j, :], xsf[:, j, :], col("d_skip", j),
                                                          o.t[:, :], ALU.mult, ALU.add))
                o.free = [k]
                V.wait(k, ztok[j])
                ytok[j] = V.do(lambda e: e.tensor_tensor(xsf[:, j, :], xsf[:, j, :], z[:, j, :], ALU.mult))

        ytok = {}

        def y_out(j):
            n2.square(xsf[:, j, :], ytok[j])
            split(YP, j, xsf[:, j, :], ytok[j], col("ssd_norm", j))
            if j:
                n2.sum_step()

        R1.flush()
        psr.bufs, saved = PS[0:5], psr.bufs
        t_scr = [V.now(), PL.now(), AC.now()]
        for b in pads.bufs + ss:
            b = Buf(b.t[:, 0:512])
            b.free = t_scr
            tmp.bufs.append(b)
        tmp.i = 0
        for h in range(18):
            if h < 3:
                z_job(5 + h)
            elif h == 3:
                R1.flush()
            if h < 16:
                head_a(h)
            if 1 <= h < 17:
                head_m(h - 1)
            if h >= 2:
                head_b(h - 2)
            if h >= 4 and h % 2 == 0:
                y_out(h // 2 - 2)
        y_out(7)
        n2.sum_step()
        del tmp.bufs[4:]
        tmp.i = 0
        psr.bufs = saved
        AC.wait(PE.now(), PL.now())
        V.wait(PE.now(), PL.now())
        XB.free = [[AC.now(), V.now()] for _ in XB.free]
        stats, chunk = memory(ytok[7])
        R2 = Runner(n2)
        for o in range(8):
            def leave(bank, tok, o=o):
                add_scaled(o, bank, tok, n2)
                after(o)
            R2.push(lambda b, o=o: project(f"os{o}", YP, b), leave)
            if o == 3:
                stats()
            if o >= 5:
                for k in range(3 * o - 15, min(3 * o - 12, 8)):
                    chunk(k)
        release(YP)
        R2.flush()

    MEM = {}

    def memory(free):
        mst = Phase(PH0 + 92672, "mm").sb("mst", [128, 8])
        mt = Phase(PH0 + 4 * 8 * S * 4 + 8192, "mm").sb("mt", [128, 2, D])
        ph = Phase(PH0 + 4 * 8 * S * 2, "mm")
        mp = MEM["pair"] = Pair(ph.sb("mh", [128, 8, ML], R), ph.sb("ml", [128, 8, ML], R), 8)
        d_mem = dsem("d_mem")
        SP.wait(free)
        t = SP.dma(d_mem, lambda e: e.dma_start(mt[:, :, :], A["mem"][0].rearrange("(i p) d -> p i d", p=128)))

        def stats():
            scr = tmp.next()
            scr.take(AC)
            AC.wait(t)
            for i in range(2):
                for j in range(2):
                    a = AC.do(lambda e, i=i, j=j: e.activation(scr.t[:, :], mt[:, i, 512 * j:512 * j + 512],
                                                               ACT.Square, accum_out=mst[:, 2 * i + j:2 * i + j + 1]))
                    AC.wait(a)
            V.wait(a)
            m2 = mst[:, 0:4].rearrange("p (i j) -> p i j", j=2)
            b = V.do(lambda e: e.tensor_tensor(mst[:, 4:6], m2[:, :, 0], m2[:, :, 1], ALU.add))
            AC.wait(b)
            a = AC.do(lambda e: e.activation(mst[:, 4:6], mst[:, 4:6], ACT.Sqrt, bias=EPS[1e-6], scale=1.0 / 1024))
            scr.free = [a]
            V.wait(a)
            b = V.do(lambda e: e.reciprocal(mst[:, 6:8], mst[:, 4:6]))
            V.wait(b)
            for i in range(2):
                b = V.do(lambda e, i=i: e.tensor_scalar(mt[:, i, :], mt[:, i, :], mst[:, 6 + i:7 + i], None,
                                                        ALU.mult))
            MEM["scaled"] = b

        def chunk(k):
            o = psr.next()
            tk = transposes(o, [(128 * i, 128, mt[:, i, 128 * k:128 * k + 128], con("I")) for i in range(2)],
                            [MEM["scaled"]])
            o.free = [split(mp, k, o.t[:, 0:ML], tk, col("mem_norm", k), n=ML)]
            MEM["used"] = PE.now()

        return stats, chunk

    def token_major(units, x, norm, dst, width, nt, k2, scale=None):
        banks = [psr.next() for _ in range(nt)]
        for b in banks:
            b.take(PE)
        k = 0
        for n, name in enumerate(units):
            i, wh, wl = weights(name)
            for kk in range(k2):
                PE.wait(x.tok[k])
                for t in range(nt):
                    a = (x.hi[:, k, 128 * t:128 * t + 128], x.lo[:, k, 128 * t:128 * t + 128])
                    last = n == len(units) - 1 and kk == k2 - 1
                    f = mm3(banks[t].t[:, 0:width], a, (wh[:, kk, :], wl[:, kk, :]), k == 0, last)
                    if not last and (t < nt - 1 or kk < k2 - 1):
                        PE.plain(f)
                    else:
                        tok = PE.do(f)
                        if last:
                            banks[t].done = tok
                k += 1
            spent(i, tok)
        out = None
        for t in range(nt):
            AC.wait(banks[t].done)
            if scale is None:
                out = AC.do(lambda e, t=t: e.copy(dst(t), banks[t].t[:, 0:width]))
            else:
                AC.wait(norm.rtok)
                out = AC.do(lambda e, t=t: e.activation(dst(t), banks[t].t[:, 0:width], ACT.Copy,
                                                        scale=scale[:, t:t + 1]))
            banks[t].free = [out]
        return out

    def xattn(n3, after):
        fence()
        ph = Phase(PH0, "xa")
        OP = X
        ph.at += 2 * 4 * 8 * S
        mp = MEM["pair"]
        ph.at += 2 * 4 * 8 * ML
        kT = ph.sb("kT", [128, 8, ML])
        vt = ph.sb("vt", [128, 2, D])
        q = ph.sb("q", [128, 8, S])
        pts = Ring([Buf(ph.sb(f"pt{i}", [128, 2, S])) for i in range(2)])
        Rk = Runner()
        kt = {}
        for o in range(8):
            def leave(bank, tok, o=o):
                V.wait(tok)
                kt[o] = V.do(lambda e: e.tensor_copy(kT[:, o, :], bank.t[:, 0:ML]))
                bank.free = [kt[o]]
            Rk.push(lambda b, o=o: project(f"mk{o}", mp, b, n=ML), leave)
        Rk.flush()
        for blk in range(2):
            tv = token_major([f"mv{blk}{kk}" for kk in range(4)], mp, None,
                             lambda t, blk=blk: vt[:, t, 512 * blk:512 * blk + 512], 512, 2, 2)
        V.wait(MEM["used"])
        Rq = Runner(n3)
        qt = {}
        for o in range(8):
            def leave(bank, tok, o=o):
                qt[o] = scaled(bank, tok, q[:, o, :], n3)
            Rq.push(lambda b, o=o: project(f"xq{o}", XB, b), leave)
        release(XB)
        Rq.flush()
        steps = [(h, i) for h in range(4) for i in range(4)]
        live, ptc = {}, {}
        sc = 1.0 / 16

        def sa(n):
            h, i = steps[n]
            o = psr.next()
            t = o.take(PE)
            PE.wait(qt[2 * h + 1], kt[7])
            for kk in range(2):
                f = mm(t[:, 0:ML], q[:, 2 * h + kk, 128 * i:128 * i + 128], kT[:, 2 * h + kk, :], kk == 0, kk == 1)
                if kk == 0:
                    PE.plain(f)
            k = PE.do(f)
            c = sm.next()
            w = c.take(V)
            V.wait(k)
            k = V.do(lambda e: e.reduce_max(w[:, 0:1], t[:, 0:ML], AX.X))
            V.wait(k)
            k = V.do(lambda e: e.tensor_scalar(w[:, 1:2], w[:, 0:1], -sc, None, ALU.mult))
            p = tmp.next()
            pt = p.take(AC)
            AC.wait(k)
            k = AC.do(lambda e: e.activation(pt[:, 0:ML], t[:, 0:ML], ACT.Exp, bias=w[:, 1:2], scale=sc,
                                             accum_out=w[:, 2:3]))
            o.free = [k]
            V.wait(k)
            k = V.do(lambda e: e.reciprocal(w[:, 3:4], w[:, 2:3]))
            V.wait(k)
            k = V.do(lambda e: e.tensor_scalar(pt[:, 0:ML], pt[:, 0:ML], w[:, 3:4], None, ALU.mult))
            c.free = [k]
            live[n] = (p, k)

        def sb_(n):
            h, i = steps[n]
            p, k = live.pop(n)
            o = psr.next()
            k = transposes(o, [(128 * j, 128, p.t[:, 128 * j:128 * j + 128], con("I")) for j in range(2)], [k])
            p.free = [k]
            if i == 0:
                ptc["b"] = pts.next()
                ptc["b"].take(V)
            P_ = ptc["b"]
            V.wait(k)
            k = V.do(lambda e, o=o: e.tensor_copy(P_.t[:, :, 128 * i:128 * i + 128],
                                             o.t[:, 0:256].rearrange("p (j t) -> p j t", j=2)))
            o.free = [k]
            if i == 3:
                held.append((n + 4, lambda: pv(h, P_, k)))

        def pv(h, P_, k):
            PE.wait(k, tv)
            for m in range(2):
                o = psr.next()
                t = o.take(PE)
                cc = 2 * h + m
                PE.plain(mm(t[:, :], vt[:, 0, 128 * cc:128 * cc + 128], P_.t[:, 0, :], True, False))
                kk = PE.do(mm(t[:, :], vt[:, 1, 128 * cc:128 * cc + 128], P_.t[:, 1, :], False, True))
                def out(o=o, cc=cc, kk=kk):
                    o.free = [split(OP, cc, o.t[:, :], kk)]
                outs.append(out)
            P_.free = [kk]

        held, outs = [], []
        for n in range(16):
            sa(n)
            while outs:
                outs.pop(0)()
            if n >= 2:
                sb_(n - 2)
            while held and n >= held[0][0]:
                held.pop(0)[1]()
        sb_(14)
        sb_(15)
        held.pop()[1]()
        while outs:
            outs.pop(0)()
        Ro = Runner()
        for o in range(8):
            def leave(bank, tok, o=o):
                bank.free = [add_h(o, bank.t[:, :], tok)]
                after(o)
            Ro.push(lambda b, o=o: project(f"xo{o}", OP, b), leave)
        release(OP)
        Ro.flush()

    def ffn(tag, groups, x, norm, at, after, gated):
        fence()
        ph = Phase(at, f"f{tag}")
        hid = [Pair(ph.sb(f"h{i}", [128, 4, S], R), ph.sb(f"l{i}", [128, 4, S], R), 4) for i in range(2)]
        Rf = Runner(norm)
        sil, cell = {}, {}

        def gate_leave(c):
            def g(bank, tok):
                b = tmp.next()
                t = b.take(V)
                k = scaled(bank, tok, t[:, :], norm)
                AC.wait(k)
                sil[c] = (b, AC.do(lambda e: e.activation(t[:, :], t[:, :], ACT.Silu)))
            return g

        def up_leave(c, pair, k_):
            def g(bank, tok):
                b = tmp.next()
                t = b.take(V)
                k = scaled(bank, tok, t[:, :], norm)
                b2, s_ = sil.pop(c)
                V.wait(k, s_)
                k = V.do(lambda e: e.tensor_tensor(t[:, :], t[:, :], b2.t[:, :], ALU.mult))
                b2.free = [k]
                b.free = [split(pair, k_, t[:, :], k)]
            return g

        def relu_leave(c, pair, k_):
            def g(bank, tok):
                b = tmp.next()
                t = b.take(V)
                k = scaled(bank, tok, t[:, :], norm)
                V.wait(k)
                k = V.do(lambda e: e.scalar_tensor_tensor(t[:, :], t[:, :], 0.0, t[:, :], ALU.max, ALU.mult))
                b.free = [split(pair, k_, t[:, :], k)]
            return g

        for kind, g in ffn_order(groups):
            pair, c0 = hid[g % 2], sum(groups[:g])
            if kind == "up":
                for c in range(c0, c0 + groups[g]):
                    if gated:
                        Rf.push(lambda b, c=c: project(f"{tag}g{c}", x, b), gate_leave(c))
                        Rf.push(lambda b, c=c: project(f"{tag}u{c}", x, b), up_leave(c, pair, c - c0))
                    else:
                        Rf.push(lambda b, c=c: project(f"{tag}u{c}", x, b), relu_leave(c, pair, c - c0))
                if g == len(groups) - 1:
                    release(x)
            else:
                n = groups[g]
                for o in range(8):
                    def f(b, o=o):
                        per = 8 // n
                        if o % per == 0:
                            cell["u"] = weights(f"{tag}d{g}_{o // per}")
                        return project(cell["u"], pair, b, nk=n, c=128 * (o % per))

                    def leave(bank, tok, o=o, g=g):
                        bank.free = [add_h(o, bank.t[:, :], tok)]
                        return after(o) if g == len(groups) - 1 else None
                    Rf.push(f, leave)
                release(pair)
        Rf.flush()

    def stick(x, norm, OPx, after):
        fence()
        ph = Phase(PH0, "st")
        q = ph.sb("q", [128, 8, S])
        kk_ = ph.sb("k", [128, 8, S])
        vt = ph.sb("v", [128, 4, D])
        OFF = [0, 512, 1024, 896]
        BK = [0, 1, 2, 1]
        wd = [512 - 128 * j for j in range(4)]
        W = [512, 512, 256]

        def sl(n):
            return slice(512 * n, 512 * n + W[n])

        Lp = Ring([Buf(ph.sb(f"L{i}", [128, 1280])) for i in range(3)])
        Ab = Ring([Buf(ph.sb(f"A{i}", [128, 512])) for i in range(2)])
        Lh = Ring([Buf(ph.sb(f"Lh{i}", [128, 1280], R)) for i in range(2)])
        Ll = Ring([Buf(ph.sb(f"Ll{i}", [128, 1280], R)) for i in range(2)])
        Rq = Runner(norm)
        qt = {}
        for o in range(16):
            def leave(bank, tok, o=o):
                V.wait(tok, norm.tok)
                if o < 8:
                    qt[o] = V.do(lambda e: e.scalar_tensor_tensor(q[:, o, :], bank.t[:, :], 0.125, rs.t[:, :],
                                                                  ALU.mult, ALU.mult))
                    bank.free = [qt[o]]
                    rs.free = [qt[o]]
                else:
                    qt[o] = scaled(bank, tok, kk_[:, o - 8, :], norm)
            Rq.push(lambda b, o=o: project(f"sq{o}", x, b), leave)
        Rq.flush()
        for blk in range(2):
            tv = token_major([f"sv{blk}{c}" for c in range(4)], x, norm,
                             lambda t, blk=blk: vt[:, t, 512 * blk:512 * blk + 512], 512, 4, 2, norm.inv)
        release(x)
        t_first = spread(n_1.inv, n_1.rtok, tmp.next())
        psr.bufs, saved = PS[0:6], psr.bufs
        AC.plain(lambda e: e.preload_act_table_set("natural_log_exp_and_others"))
        live = {}
        ob = {}

        def a_(h):
            p0 = 64 * (h % 2)
            c = h // 2
            bk = [psr.next() for _ in range(3)]
            for b in bk:
                b.take(PE)
            PE.wait(qt[c], qt[8 + c])
            for j in (2, 1, 3, 0):
                t = bk[BK[j]].t[:, OFF[j] % 512:OFF[j] % 512 + wd[j]]
                f = mm(t, kk_[p0:p0 + 64, c, 128 * j:128 * j + 128], q[p0:p0 + 64, c, 128 * j:512],
                       j != 3, False)
                if j in (1, 2):
                    PE.plain(f)
                elif j == 3:
                    k1 = PE.do(f)
            k = PE.do(f)
            L, Abf = Lp.next(), Ab.next()
            l, a = L.take(V, AC), Abf.take(V, AC)
            V.wait(k)
            AC.wait(k1)
            V.wait(V.do(lambda e: e.tensor_scalar(l[:, 0:512], bk[0].t[:, :], 0.0, None, ALU.max)))
            d = V.do(lambda e: e.scalar_tensor_tensor(a[:, :], l[:, 0:512], 2.0, bk[0].t[:, :], ALU.mult,
                                                      ALU.subtract))
            ln = {}
            for n in (1, 2):
                k = AC.do(lambda e, n=n: e.activation(l[:, sl(n)], bk[n].t[:, 0:W[n]], ACT.Abs))
            AC.wait(k)
            k = AC.do(lambda e: e.activation(l[:, 512:1280], l[:, 512:1280], ACT.Exp, scale=-1.0))
            AC.wait(k)
            ln[1] = ln[2] = AC.do(lambda e: e.activation(l[:, 512:1280], l[:, 512:1280], ACT.Ln, bias=ONE1))
            live[h] = (bk, L, Abf, ln)

            def rest():
                AC.wait(d)
                k = AC.do(lambda e: e.activation(a[:, :], a[:, :], ACT.Exp, scale=-1.0))
                AC.wait(k)
                ln[0] = AC.do(lambda e: e.activation(a[:, :], a[:, :], ACT.Ln, bias=ONE1))
            return rest

        def b_(h):
            bk, L, hb, lb, k = live[h]
            for j in (3, 2, 1, 0):
                t = bk[BK[j]].t
                o = OFF[j] % 512
                PE.wait(k[BK[j]])
                if j == 1:
                    PE.wait(k[2])
                PE.plain(mm(t[:, o:o + 128], Ib[:, :], maskb[:, 2, :], False, False))
                for i in range(j, 4):
                    out = t[:, o + 128 * (i - j):o + wd[j]]
                    for part in (hb.t, lb.t):
                        f = mm(out, trir[:, 0 if i == j else 1, :], part[:, OFF[i]:OFF[i] + wd[i]], False,
                               i == 3 and part is lb.t)
                        if not (i == 3 and part is lb.t):
                            PE.plain(f)
                d = PE.do(f)
                if j != 3:
                    n = BK[j]
                    AC.wait(d)
                    w_ = AC.do(lambda e, n=n: e.activation(L.t[:, sl(n)], bk[n].t[:, 0:W[n]], ACT.Exp))
                    bk[n].free = [w_]
            hb.free = [d]
            lb.free = [d]
            live[h] = (L, w_)

        def a2_(h):
            bk, L, Abf, ln = live[h]
            l, a = L.t, Abf.t
            hb, lb = Lh.next(), Ll.next()
            hi, lo = hb.take(PL), lb.take(V)
            k = {}
            hd = {}

            def low(n):
                V.wait(hd[n])
                k[n] = V.do(lambda e: e.tensor_tensor(lo[:, sl(n)], l[:, sl(n)], hi[:, sl(n)].bitcast(F),
                                                      ALU.subtract))

            for n in (1, 2, 0):
                V.wait(ln[n])
                if n:
                    d = V.do(lambda e, n=n: e.scalar_tensor_tensor(l[:, sl(n)], bk[n].t[:, 0:W[n]], 0.0,
                                                                   l[:, sl(n)], ALU.max, ALU.add))
                else:
                    d = V.do(lambda e: e.tensor_tensor(l[:, 0:512], l[:, 0:512], a[:, :], ALU.add))
                V.wait(d)
                for j in range(4):
                    if BK[j] == n:
                        m = V.do(lambda e, j=j: e.tensor_tensor(l[:, OFF[j]:OFF[j] + 128],
                                                                l[:, OFF[j]:OFF[j] + 128], con("MS"), ALU.mult))
                PL.wait(m)
                hd[n] = PL.do(lambda e, n=n: e.tensor_scalar(hi[:, sl(n)], l[:, sl(n)], 1.0, 0.0, ALU.mult,
                                                             ALU.add))
                if n != 1:
                    low({2: 1, 0: 2}[n])
            low(0)
            Abf.free = [m]
            live[h] = (bk, L, hb, lb, k)

        def c_(h):
            L, d = live.pop(h)
            p0 = 64 * (h % 2)
            if h % 2 == 0:
                ob[0] = PS[6 + (h // 2) % 2]
                ob[0].take(PE)
            o = ob[0]
            PE.wait(d, tv)
            for j in range(4):
                f = mm(o.t[p0:p0 + 64, 128 * j:512], vt[:, j, 64 * h:64 * h + 64], L.t[:, OFF[j]:OFF[j] + wd[j]],
                       j == 0, j == 3)
                if j < 3:
                    PE.plain(f)
            k = PE.do(f)
            L.free = [k]
            if h % 2:
                def out():
                    o.free = [split(OPx, h // 2, o.t[:, :], k)]
                return out
            return None

        out = None
        for h in range(16):
            if h >= 1:
                a2_(h - 1)
            if out:
                out()
            if 3 <= h < 11:
                first_end(h - 3, t_first)
            rest = a_(h)
            out = c_(h - 2) if h >= 2 else None
            if h >= 1:
                b_(h - 1)
            rest()
        a2_(15)
        out()
        c_(14)
        b_(15)
        c_(15)()
        psr.bufs = saved
        fence()
        Ro = Runner()
        for o in range(8):
            def leave(bank, tok, o=o):
                bank.free = [add_h(o, bank.t[:, :], tok)]
                after(o)
            Ro.push(lambda b, o=o: project(f"so{o}", OPx, b), leave)
        release(OPx)
        Ro.flush()

    def nsa(xkv, xq, norm, OPx, after):
        fence()
        ph = Phase(PH0 + 8 * S * 8, "ns")
        q = ph.sb("q", [128, 8, S])
        vs = [ph.sb("vs", [128, 4, 256]), ph.sb("vw", [128, 4, 256])]
        gat = ph.sb("gat", [128, 4, 48])
        kc = ph.sb("kc", [128, 4, 31])
        vc = ph.sb("vc", [31, 4, 64])
        ptc = Buf(ph.sb("ptc", [31, S]))
        r3 = ph.at
        rope = ph.sb("rope", [128, 2, S])
        w2 = ph.sb("w2", [128, 2, 2, 2, 64])
        rmat = ph.sb("rmat", [128, 5, 128])
        hdn = ph.sb("hdn", [128, 2, 2, 124])
        cm = Ring([Buf(ph.sb(f"cw{i}", [128, 124])) for i in range(6)])
        r4 = ph.at
        d_c = dsem("d_cmp")
        tw = None
        for c in range(2):
            for dup in range(2):
                tw = SP.dma(d_c, lambda e, c=c, dup=dup: e.dma_start(
                    w2[:, c, :, dup, :], A["cmp_w2_2"][c].rearrange("(k p) d -> p k d", p=128)))
        a0 = CONST["P"][0]
        tw = SP.dma(d_c, lambda e: e.dma_start(rmat[:, :, :], const_d[:, a0:a0 + 640].rearrange("p (k n) -> p k n", k=5)))
        tw = SP.dma(d_c, lambda e: e.dma_start(rope[:, :, :], const_d[:, a0 + 640:a0 + 1664].rearrange("p (k n) -> p k n", k=2)))
        RCt, RSt = rope[:, 0, :], rope[:, 1, :]
        Rq = Runner(norm)
        qt, qrt = {}, {}
        for o in range(8):
            def leave(bank, tok, o=o):
                qt[o] = scaled(bank, tok, q[:, o, :], norm)
            Rq.push(lambda b, o=o: project(f"nq{o}", xq, b), leave)

        def g_leave(bank, tok):
            b = tmp.next()
            t = b.take(V)
            a = scaled(bank, tok, t[0:48, :], norm, p=48)

            def late():
                o = psr.next()
                k = transposes(o, [(48 * i, 128, t[0:48, 128 * i:128 * i + 128], con("I", 0, 48, 0, 48))
                                   for i in range(4)], [a])
                b.free = [k]
                V.wait(k)
                k = V.do(lambda e: e.tensor_tensor(
                    gat[:, :, :], o.t[:, 0:192].rearrange("p (i c) -> p i c", i=4),
                    col("gate_b", 0, 48).unsqueeze(1).to_broadcast([128, 4, 48]), ALU.add))
                o.free = [k]
                AC.wait(k)
                k = AC.do(lambda e: e.activation(gat[:, :, :], gat[:, :, :], ACT.Exp, scale=-1.0))
                V.wait(k)
                k = V.do(lambda e: e.tensor_scalar(gat[:, :, :], gat[:, :, :], 1.0, None, ALU.add))
                V.wait(k)
                V.do(lambda e: e.reciprocal(gat[:, :, :], gat[:, :, :]))
            return late

        Rq.push(lambda b: project("ng", xq, b, m=48), g_leave)
        Rq.flush()
        fence()
        pk = Phase(PH0, "nk")
        X2 = pk.sb("x2", [128, 2, 4, 512])
        kd = [pk.sb("ks", [128, 4, S]), pk.sb("kw", [128, 4, S])]
        pts = Phase(PH0, "nt").sb("pts", [128, 2, 4, S])
        ph2 = Phase(ph.at, "nq")
        qr = ph2.sb("qr", [128, 8, S])
        PTS = Buf(pts)
        PE.wait(tw)
        V.wait(tw)
        PL.wait(tw)
        Rk = Runner()
        x2t = []
        for o in range(4):
            def leave(bank, tok, o=o):
                c, g0 = o // 2, 2 * (o % 2)
                V.wait(tok, norm.tok)
                for g in range(2):
                    s0 = 64 * g
                    k = V.do(lambda e, g=g, s0=s0: e.tensor_tensor(
                        X2[0:64, c, g0 + g, :], bank.t[s0:s0 + 64, :], rs.t[0:64, :], ALU.mult))
                    k = V.do(lambda e, g=g, s0=s0: e.tensor_tensor(
                        X2[64:128, c, g0 + g, 0:511], bank.t[s0:s0 + 64, 1:512], rs.t[0:64, 1:512], ALU.mult))
                bank.free = [k]
                rs.free = [k]
                x2t.append(k)
            Rk.push(lambda b, o=o: project(f"nc{o}", xkv, b), leave)
        kdt = {}

        def rotate(src, tok, mats, dst, rel, key):
            PE.wait(tok)
            o1 = None
            if mats[0] is not None:
                o1 = psr.next()
                PE.plain(mm(o1.take(PE)[:, :], mats[0], src, True, True))
            o2 = psr.next()
            k = PE.do(mm(o2.take(PE)[:, :], mats[1], src, True, True))
            b = sqr.next()
            bt = b.take(V)
            V.wait(k, tok)
            s1 = src if o1 is None else o1.t[:, :]
            a = V.do(lambda e: e.tensor_tensor(dst, s1, RCt, ALU.mult))
            c = V.do(lambda e: e.tensor_tensor(bt[:, :], o2.t[:, :], RSt, ALU.mult))
            if o1 is not None:
                o1.free = [a]
            o2.free = [c]
            PL.wait(a, c)
            kdt[key] = PL.do(lambda e: e.tensor_tensor(dst, dst, bt[:, :], ALU.add))
            b.free = [kdt[key]]
            return k

        for kind in range(2):
            for o in range(2):
                def leave(bank, tok, kind=kind, o=o):
                    b = tmp.next()
                    t = b.take(V)
                    a = scaled(bank, tok, t[:, :], norm)

                    def late():
                        for g in range(2):
                            k = rotate(t[:, :], a, (rmat[:, 1 + g, :], rmat[:, 3 + g, :]),
                                       kd[kind][:, 2 * o + g, :], None, ("k", kind, 2 * o + g))
                        b.free = [k]
                    return late
                Rk.push(lambda b, kind=kind, o=o: project(f"nk{kind}{o}", xkv, b), leave)
        Rk.drain()
        for kind in range(2):
            tv = token_major([f"nv{kind}{c}" for c in range(2)], xkv, norm,
                             lambda t, kind=kind: vs[kind][:, t, :], 256, 4, 4, norm.inv)
            Rk.later(-1000)
        release(xkv)
        for o in range(8):
            rotate(q[:, o, :], qt[o], (None, rmat[:, 0, :]), qr[:, o, :], None, ("q", o))
        cops = []
        AC.wait(*x2t)

        def window_in(n):
            b = cm.next()
            t = b.take(AC)
            cops.append((b, AC.do(lambda e: e.activation(
                t[:, :].rearrange("p (g n) -> p g n", g=4), X2[:, n // 16, :, 2 * (n % 16):2 * (n % 16) + 481:16],
                ACT.Identity, bias=col("cmp_pos", n)))))

        for n in range(4):
            window_in(n)
        for n in range(32):
            c, j = n // 16, n % 16
            if j == 0:
                bk = [psr.next(), psr.next()]
                for b in bk:
                    b.take(PE)
            if j % 4 == 0:
                i, w = weights(f"c1{c}{j // 4}")
            if n + 4 < 32:
                window_in(n + 4)
            b, k = cops[n]
            PE.wait(k)
            for m in range(2):
                f = mm(bk[m].t[:, 0:124], w[:, j % 4, 128 * m:128 * m + 128], b.t[:, :], j == 0, j == 15)
                if m == 0:
                    PE.plain(f)
            k = PE.do(f)
            b.free = [k]
            if j % 4 == 3:
                spent(i, k)
            if j == 15:
                AC.wait(k)
                for m in range(2):
                    th = AC.do(lambda e, c=c, m=m, bk=bk: e.activation(hdn[:, c, m, :], bk[m].t[:, 0:124],
                                                                       ACT.Gelu_apprx_tanh))
                    bk[m].free = [th]
        o = psr.next()
        t = o.take(PE)
        PE.wait(th, tw)
        for m in range(2):
            f = mm(t[:, 0:124], w2[:, 0, m, :, :].rearrange("p a d -> p (a d)"), hdn[:, 0, m, :], m == 0, m == 1)
            if m == 0:
                PE.plain(f)
        k = PE.do(f)
        V.wait(k)
        tkc = V.do(lambda e, t=t: e.tensor_copy(kc[:, :, :], t[:, 0:124].rearrange("p (g n) -> p g n", g=4)))
        o.free = [tkc]
        o = psr.next()
        t = o.take(PE)
        for g in range(4):
            for m in range(2):
                f = mm(t[0:31, 64 * g:64 * g + 64], hdn[:, 1, m, 31 * g:31 * g + 31], w2[:, 1, m, 0, :],
                       g == 0 and m == 0, m == 1)
                if not (g == 3 and m == 1):
                    PE.plain(f)
        k = PE.do(f)
        V.wait(k)
        tvc = V.do(lambda e, t=t: e.tensor_copy(vc[:, :, :], t[0:31, 0:256].rearrange("p (g n) -> p g n", g=4)))
        o.free = [tvc]
        fence()
        pe = Phase(r3, "ne")
        tmp.bufs = tmp.bufs + [Buf(pe.sb(f"t{i}", [128, S])) for i in range(6)]
        tmp.i = 0
        assert pe.at <= r4
        sc = 0.125
        scr, ptr = Ring(PS[0:4]), Ring(PS[4:6])
        steps = []
        for h in range(16):
            steps.append((h, -1))
            for i in (3, 2, 1, 0):
                steps.append((h, i))
        live, ob, held, outs = {}, {}, [], []

        def a_(n):
            h, i = steps[n]
            g, c, p0 = h // 4, h // 2, 64 * (h % 2)
            w_ = sm.next()
            w = w_.take(V)
            PE.wait(kdt[("q", c)])
            if i < 0:
                o = scr.next()
                t = o.take(PE)
                PE.wait(tkc)
                for ti in range(4):
                    f = mm(t[:, 32 * ti:32 * ti + 31], q[p0:p0 + 64, c, 128 * ti:128 * ti + 128],
                           kc[p0:p0 + 64, g, :], ti == 0, False)
                    PE.plain(f)
                k = PE.do(mm(t[:, 0:128].rearrange("p (i n) -> p i n", i=4)[:, :, 0:31], Ib[:, :],
                             maskb[:, 3, :].rearrange("p (i n) -> p i n", i=4)[:, :, 0:31], False, True))
                tv_ = t[:, 0:128].rearrange("p (i n) -> p i n", i=4)[:, :, 0:31]
                p = tmp.next()
                pt = p.take(V)
                pv = pt[:, 0:128].rearrange("p (i n) -> p i n", i=4)[:, :, 0:31]
                V.wait(k)
                k = V.do(lambda e: e.tensor_reduce(w[:, 0:4], tv_, AX.X, ALU.max))
                V.wait(k)
                k = V.do(lambda e: e.tensor_tensor(pv, tv_, w[:, 0:4].unsqueeze(2).to_broadcast([128, 4, 31]),
                                                   ALU.subtract))
                o.free = [k]
                AC.wait(k)
                k = AC.do(lambda e: e.activation(pv, pv, ACT.Exp, scale=sc))
                live[n] = (w_, k, p, pv)
                return
            N = 128 * (i + 1)
            bks = []
            for kind in range(2):
                o = scr.next()
                t = o.take(PE)
                PE.wait(kdt[("k", kind, g)])
                PE.plain(mm(t[:, 0:N], qr[p0:p0 + 64, c, 128 * i:128 * i + 128], kd[kind][p0:p0 + 64, g, 0:N],
                            True, False))
                k = PE.do(mm(t[:, N - 128:N], Ib[:, :], maskb[:, 1, :], False, True))
                bks.append((o, t))
                V.wait(k)
                k = V.do(lambda e, kind=kind, t=t: e.reduce_max(w[:, kind:kind + 1], t[:, 0:N], AX.X))
            V.wait(k)
            k = V.do(lambda e: e.tensor_scalar(w[:, 2:4], w[:, 0:2], -sc, None, ALU.mult))
            AC.wait(k)
            ps_ = []
            for kind in range(2):
                o, t = bks[kind]
                p = tmp.next()
                pt = p.take(AC)
                k = AC.do(lambda e, kind=kind, t=t, pt=pt: e.activation(
                    pt[:, 0:N], t[:, 0:N], ACT.Exp, bias=w[:, 2 + kind:3 + kind], scale=sc,
                    accum_out=w[:, 4 + kind:5 + kind]))
                o.free = [k]
                ps_.append((p, pt))
            live[n] = (w_, k, ps_)

        def a2_(n):
            h, i = steps[n]
            w_, k = live[n][0:2]
            w = w_.t
            V.wait(k)
            if i < 0:
                p, pv = live[n][2:4]
                k = V.do(lambda e: e.tensor_reduce(w[:, 4:8], pv, AX.X, ALU.add))
                V.wait(k)
                k = V.do(lambda e: e.reciprocal(w[:, 8:12], w[:, 4:8]))
                V.wait(k)
                k = V.do(lambda e: e.tensor_tensor(w[:, 12:16], w[:, 8:12], gat[:, :, h], ALU.mult))
                V.wait(k)
                k = V.do(lambda e: e.tensor_tensor(pv, pv, w[:, 12:16].unsqueeze(2).to_broadcast([128, 4, 31]),
                                                   ALU.mult))
                w_.free = [k]
                live[n] = [(p, k)]
                return
            N = 128 * (i + 1)
            ps_ = live[n][2]
            out = []
            k = V.do(lambda e: e.reciprocal(w[:, 6:8], w[:, 4:6]))
            V.wait(k)
            k = V.do(lambda e: e.tensor_tensor(w[:, 8:10], w[:, 6:8], gat[:, i, 16 + h:16 + h + 17:16], ALU.mult))
            V.wait(k)
            for kind in range(2):
                p, pt = ps_[kind]
                k = V.do(lambda e, kind=kind, pt=pt: e.tensor_scalar(pt[:, 0:N], pt[:, 0:N], w[:, 8 + kind:9 + kind],
                                                                     None, ALU.mult))
                out.append((p, k))
            w_.free = [k]
            live[n] = out

        def b_(n):
            h, i = steps[n]
            g, c, p0 = h // 4, h // 2, 64 * (h % 2)
            if i < 0:
                (p, k), = live.pop(n)
                o = ptr.next()
                k = transposes(o, [(128 * ti, 31, p.t[:, 32 * ti:32 * ti + 31], con("I")) for ti in range(4)], [k])
                p.free = [k]
                ptc.take(AC)
                AC.wait(k, t_z)
                k = AC.do(lambda e: e.copy(ptc.t[:, 31:S], o.t[0:31, 31:S]))
                o.free = [k]
                if h % 2 == 0:
                    ob[0] = PS[6 + (h // 2) % 2]
                    ob[0].take(PE)

                def pv(o=ob[0], k=k):
                    PE.wait(k, tvc)
                    ptc.free = [PE.do(mm(o.t[p0:p0 + 64, :], vc[:, g, :], ptc.t[:, :], True, False))]
                held.append(pv)
                return
            for kind, (p, k) in enumerate(live.pop(n)):
                o = ptr.next()
                k = transposes(o, [(128 * j, 128, p.t[:, 128 * j:128 * j + 128], con("I")) for j in range(i + 1)], [k])
                p.free = [k]
                Q = (AC, V)[kind]
                if i == 3:
                    if kind == 0:
                        PTS.take(AC)
                        V.wait(PTS.was)
                Q.wait(k)
                dst = pts[:, kind, 0:i + 1, 128 * i:128 * i + 128]
                src = o.t[:, 0:128 * (i + 1)].rearrange("p (j t) -> p j t", t=128)
                k = Q.do((lambda e, dst=dst, src=src: e.copy(dst, src)) if kind == 0 else
                         (lambda e, dst=dst, src=src: e.tensor_copy(dst, src)))
                o.free = [k]
                live.setdefault("pt", []).append(k)
            if i == 0:
                def pv(o=ob[0], ks=live.pop("pt")):
                    PE.wait(tv, *ks)
                    for kind in range(2):
                        for j in range(4):
                            f = mm(o.t[p0:p0 + 64, 128 * j:512], vs[kind][:, j, 64 * g:64 * g + 64],
                                   pts[:, kind, j, 128 * j:512], False, kind == 1 and j == 3)
                            if not (kind == 1 and j == 3):
                                PE.plain(f)
                    k = PE.do(f)
                    PTS.free = [k]
                    PTS.was = k
                    if h % 2:
                        def out():
                            o.free = [split(OPx, c, o.t[:, :], k)]
                        outs.append((n + 4, out))
                held.append(pv)

        PTS.was = None
        t_z = V.do(lambda e: e.memset(ptc.t[:, 0:31], 0.0))
        PE.wait(t_z)
        for n in range(len(steps)):
            was = held[:]
            held.clear()
            a_(n)
            for f in was:
                f()
            if n >= 3:
                b_(n - 3)
            if n >= 1:
                a2_(n - 1)
            while outs and n >= outs[0][0]:
                outs.pop(0)[1]()
        a2_(len(steps) - 1)
        for n in (3, 2, 1):
            b_(len(steps) - n)
            while held:
                held.pop(0)()
        while outs:
            outs.pop(0)[1]()
        del tmp.bufs[4:]
        Ro = Runner()
        fence()
        for o in range(8):
            def leave(bank, tok, o=o):
                bank.free = [add_h(o, bank.t[:, :], tok)]
                after(o)
            Ro.push(lambda b, o=o: project(f"no{o}", OPx, b), leave)
        release(OPx)
        Ro.flush()

    hg = Phase(PH0 + 4 * 8 * S * 4, "fi").sb("hg", [128, 8, S])
    ot = Phase(PH0, "fi").sb("ot", [128, 4, D])

    def last(k):
        hread[k] = [n_9.square(H[:, k, :], htok[k])]
        AC.wait(htok[k])
        a = AC.do(lambda e: e.activation(hg[:, k, :], H[:, k, :], ACT.Copy, scale=col("final", k)))
        while n_9.k < len(n_9.sq) - 1:
            n_9.sum_step()

        def late():
            o = psr.next()
            t = transposes(o, [(128 * i, 128, hg[:, k, 128 * i:128 * i + 128], con("I")) for i in range(4)], [a])
            q = (AC, V)[k % 2]
            q.wait(t)
            dst = ot[:, :, 128 * k:128 * k + 128]
            src = o.t[:, :].rearrange("p (i c) -> p i c", i=4)
            if k % 2:
                t = V.do(lambda e: e.tensor_copy(dst, src))
            else:
                t = AC.do(lambda e: e.copy(dst, src))
            o.free = [t]
            turned.append(t)
        return late

    def final():
        n_9.sum_step()
        n_9.token()
        d_out = dsem("d_out")
        for i in range(4):
            done_ = []
            for half in range(2):
                dst = ot[:, i, 512 * half:512 * half + 512]
                if half == 0:
                    AC.wait(n_9.rtok, *turned)
                    t = AC.do(lambda e, i=i, dst=dst: e.activation(dst, dst, ACT.Copy, scale=n_9.inv[:, i:i + 1]))
                else:
                    V.wait(n_9.rtok, *turned)
                    t = V.do(lambda e, i=i, dst=dst: e.tensor_scalar(dst, dst, n_9.inv[:, i:i + 1], None, ALU.mult))
                done_.append(t)
            SP.wait(*done_)
            t_out = SP.dma(d_out, lambda e, i=i: e.dma_start(out_d[0, 128 * i:128 * i + 128, :], ot[:, i, :]))
        SP.wait(t_out)

    n_x = Norm(1e-6)
    n_f = Norm(1e-6)
    n_1 = Norm(1e-6)
    n_sb = TwoNorms(n_1)
    n_m0 = Norm(1e-5)
    n_ns = Norm(1e-5)
    n_m1 = Norm(1e-5)

    n_9 = Norm(1e-5)

    turned = []

    def nothing(k):
        pass

    def before_stick(k):
        hread[k] = [n_sb.square(H[:, k, :], htok[k])]
        hread[k].append(split(X, k, H[:, k, :], htok[k], g12[:, k:k + 1]))
        while n_sb.k < len(n_1.sq) - 1:
            n_sb.sum_step()

    def first_end(k, tok):
        AC.wait(htok[k], *hread[k])
        t = AC.do(lambda e: e.activation(H[:, k, :], H[:, k, :], ACT.Copy, scale=col("first", k)))
        PL.wait(t, tok)
        htok[k] = PL.do(lambda e: e.tensor_tensor(H[:, k, :], H[:, k, :], rs.t[:, :], ALU.mult))
        hread[k] = []
        rs.free = [htok[k]]

    f_kv, f_q = None, None

    def both(k):
        hread[k] = [n_ns.square(H[:, k, :], htok[k])]
        hread[k].append(split(X, k, H[:, k, :], htok[k], col("kv_norm", k)))
        hread[k].append(split(XB, k, H[:, k, :], htok[k], col("ng", 16 + k)))
        while n_ns.k < len(n_ns.sq) - 1:
            n_ns.sum_step()

    def run_all():
        mixer(nothing if stop == "mixer" else normed(n_x, "xattn_norm", x=XB))
        if stop == "mixer":
            return
        xattn(n_x, nothing if stop == "xattn" else normed(n_f, "ffn_norm", x=XB))
        if stop == "xattn":
            return
        ffn("f", GU, XB, n_f, PH0 + 8 * S * 8, nothing if stop == "ffn" else before_stick, True)
        if stop == "ffn":
            return
        stick(X, n_sb, X, nothing if stop == "stick" else normed(n_m0, "ng", 8, XB))
        if stop == "stick":
            return
        ffn("m", [4] * 8, XB, n_m0, PH0 + 8 * S * 8, nothing if stop == "mlp0" else both, False)
        if stop == "mlp0":
            return
        nsa(X, XB, n_ns, X, nothing if stop == "nsa" else normed(n_m1, "ng", 24, XB))
        if stop == "nsa":
            return
        ffn("n", [4] * 8, XB, n_m1, PH0 + 8 * S * 8, last, False)

    run_all()
    if stop:
        fence()
        for k in range(8):
            last(k)()
    final()
    assert stop or at[0] == len(U)

    with nc.Block() as block:
        @block.sync
        def _(e):
            for f in SP.ops:
                f(e)

        @block.tensor
        def _(e):
            for f in PE.ops:
                f(e)

        @block.vector
        def _(e):
            for f in V.ops:
                f(e)

        @block.scalar
        def _(e):
            for f in AC.ops:
                f(e)

        @block.gpsimd
        def _(e):
            for f in PL.ops:
                f(e)


_INS = ["x", "mem", "w_in", "pool_w", "w_out_mix", "w_q", "w_kv", "w_o", "w_gate_up", "w_down",
        "sb_w_qkv_2", "sb_w_o_2", "nsa_w_kv_2", "cmp_w1_2", "cmp_w2_2", "nsa_w_q_2", "nsa_w_o_2",
        "mlp_w1_2", "mlp_w2_2"]


def columns(a):
    c = np.zeros((128, NCOLS), np.float32)

    def put(name, v):
        at, w = COLS[name]
        c[:, at:at + w] = v

    def feat(v):
        return np.asarray(v).reshape(-1, 128).T

    for name, v in (("mix_norm", a["mix_norm"]), ("conv_b", a["conv_b"]), ("ssd_norm", a["ssd_norm"]),
                    ("pool_scale", a["pool_scale"]), ("xattn_norm", a["xattn_norm"]),
                    ("mem_norm", a["mem_norm"]), ("ffn_norm", a["ffn_norm"]), ("kv_norm", a["kv_norm_2"]),
                    ("first", a["final_norm"]), ("final", a["final_norm_2"]), ("ng", a["norm_gain_2"]),
                    ("conv_w", a["conv_w"])):
        put(name, feat(v))
    put("d_skip", feat(np.repeat(np.asarray(a["d_skip"]).reshape(-1), 64)))
    pos = np.asarray(a["cmp_pos_2"]).reshape(2, 16, 2, 64)
    put("cmp_pos", pos.transpose(2, 3, 0, 1).reshape(128, 32))
    put("dt_bias", np.tile(np.asarray(a["dt_bias"]).reshape(1, 16), (128, 1)))
    put("a_log", np.tile(np.asarray(a["a_log"]).reshape(1, 16), (128, 1)))
    put("gate_b", np.tile(np.asarray(a["nsa_gate_b_2"]).reshape(1, 48), (128, 1)))
    return c


def kernel(**inputs):
    import concourse.bacc as bacc
    from concourse.bass_utils import run_bass_kernel_spmd

    nc = bacc.Bacc("TRN2", target_bir_lowering=False, num_devices=1)
    arrays = {f"in_{n}": np.ascontiguousarray(inputs[n]) for n in _INS}
    arrays["in_cols"] = columns(inputs)
    arrays["in_const"] = constants()
    aps = {n: nc.dram_tensor(n, a.shape, F, kind="ExternalInput").ap() for n, a in arrays.items()}
    out = nc.dram_tensor("out_0", (1, S, D), F, kind="ExternalOutput").ap()
    program(nc, {n: aps[f"in_{n}"] for n in _INS}, aps["in_cols"], aps["in_const"], out)
    r = run_bass_kernel_spmd(nc, [arrays], core_ids=[0])
    return r.results[0]["out_0"]
```
